# Optimizing a Trainium2 kernel written in Bass

```python
import jax, jax.numpy as jnp
from jax import lax
import numpy as np

D_MODEL = 1024
BATCH = 1
SEQ = 1024
DEPTH = 1

POOL_WINDOWS = (2, 4, 8, 16)
POOL_GROUPS = len(POOL_WINDOWS)
POOL_GROUP_DIM = D_MODEL // 8
POOL_WIDTH = POOL_GROUPS * POOL_GROUP_DIM
SGU_CHUNK = 128
SGU_HEADS = 8
SGU_WIDTH = D_MODEL
SGU_HEAD_DIM = SGU_WIDTH // SGU_HEADS
N_BRANCHES = 2
IN_WIDTH = POOL_WIDTH + 2 * SGU_WIDTH + N_BRANCHES * D_MODEL
SPLITS = (POOL_WIDTH,
          POOL_WIDTH + SGU_WIDTH,
          POOL_WIDTH + 2 * SGU_WIDTH,
          POOL_WIDTH + 2 * SGU_WIDTH + D_MODEL)
N_EXPERTS = 16
CAPACITY_FACTOR = 2
D_EXPERT = 2 * D_MODEL
ALPHA = (2 * DEPTH) ** 0.25
BETA = (8 * DEPTH) ** -0.25
LN_EPS = 1e-5

kernel_name = "hybrid_pool_sgu_ec_moe_deepnorm"

def layer_norm(x, g, b):
    xf = x.astype(jnp.float32)
    mu = jnp.mean(xf, axis=-1, keepdims=True)
    xc = xf - mu
    var = jnp.mean(xc * xc, axis=-1, keepdims=True)
    return (xc * lax.rsqrt(var + LN_EPS) * g + b).astype(x.dtype)

def multiscale_pool(a):
    S = a.shape[1]
    af = a.astype(jnp.float32)
    cs = jnp.concatenate([jnp.zeros_like(af[:, :1]), jnp.cumsum(af, axis=1)], axis=1)
    t = jnp.arange(S)
    outs = []
    for g, w in enumerate(POOL_WINDOWS):
        lo = jnp.clip(t - w // 2, 0, S)
        hi = jnp.clip(t + w // 2, 0, S)
        sl = slice(g * POOL_GROUP_DIM, (g + 1) * POOL_GROUP_DIM)
        csg = cs[:, :, sl]
        count = (hi - lo).astype(jnp.float32)[None, :, None]
        outs.append((csg[:, hi] - csg[:, lo]) / count - af[:, :, sl])
    return jnp.concatenate(outs, axis=-1).astype(a.dtype)

def spatial_gating(u, v, ln_g, ln_b, w_s, b_s):
    B, S, _ = v.shape
    v = layer_norm(v, ln_g, ln_b)
    vc = v.reshape(B, S // SGU_CHUNK, SGU_CHUNK, SGU_HEADS, SGU_HEAD_DIM)
    mixed = jnp.einsum('hpq,bcqhd->bcphd', w_s, vc) + b_s.T[None, None, :, :, None]
    return u * mixed.reshape(B, S, SGU_WIDTH)

def hybrid_mixer(h, w_in, b_in, pool_w, pool_scale, sgu_ln_g, sgu_ln_b, sgu_w, sgu_b, p_a, p_b, w_out):
    B, S, _ = h.shape
    proj = h @ w_in + b_in
    a, u, v, ga, gb = jnp.split(proj, SPLITS, axis=-1)
    pa = multiscale_pool(a).reshape(B, S, POOL_GROUPS, POOL_GROUP_DIM)
    ya = jnp.einsum('bsgc,gcd->bsgd', pa, pool_w).reshape(B, S, POOL_WIDTH) * pool_scale
    yb = spatial_gating(jax.nn.gelu(u), jax.nn.gelu(v), sgu_ln_g, sgu_ln_b, sgu_w, sgu_b)
    merged = jax.nn.sigmoid(ga) * (ya @ p_a) + jax.nn.sigmoid(gb) * (yb @ p_b)
    return merged @ w_out

def expert_choice_ffn(h, w_router, w_gate, w_up, w_down):
    B, S, D = h.shape
    cap = CAPACITY_FACTOR * S // N_EXPERTS
    affinity = jax.nn.softmax((h @ w_router).astype(jnp.float32), axis=-1)
    gates, idx = lax.top_k(jnp.swapaxes(affinity, 1, 2), cap)
    xe = jax.vmap(lambda hb, ib: hb[ib])(h, idx)
    hid = jax.nn.silu(jnp.einsum('becd,edf->becf', xe, w_gate)) * jnp.einsum('becd,edf->becf', xe, w_up)
    ye = jnp.einsum('becf,efd->becd', hid, w_down) * gates[..., None].astype(h.dtype)
    return jax.vmap(
        lambda yb, ib: jnp.zeros((S, D), yb.dtype).at[ib.reshape(-1)].add(yb.reshape(-1, D))
    )(ye, idx)

def setup_inputs(seed: int = 0) -> dict:
    key = jax.random.key(seed)
    ks = jax.random.split(key, 24)

    def nrm(k, shape, scale):
        return jax.random.normal(k, shape, jnp.float32) * scale

    L, D = DEPTH, D_MODEL
    return {
        "x": nrm(ks[0], (BATCH, SEQ, D), 1.0),
        "in_ln_g": 1.0 + nrm(ks[1], (D,), 0.01),
        "in_ln_b": nrm(ks[2], (D,), 0.01),
        "w_in": nrm(ks[3], (L, D, IN_WIDTH), D ** -0.5),
        "b_in": nrm(ks[4], (L, IN_WIDTH), 0.01),
        "pool_w": nrm(ks[5], (L, POOL_GROUPS, POOL_GROUP_DIM, POOL_GROUP_DIM), POOL_GROUP_DIM ** -0.5),
        "pool_scale": 1.0 + nrm(ks[6], (L, POOL_WIDTH), 0.1),
        "sgu_ln_g": 1.0 + nrm(ks[7], (L, SGU_WIDTH), 0.01),
        "sgu_ln_b": nrm(ks[8], (L, SGU_WIDTH), 0.01),
        "sgu_w": nrm(ks[9], (L, SGU_HEADS, SGU_CHUNK, SGU_CHUNK), 0.5 * SGU_CHUNK ** -0.5),
        "sgu_b": 1.0 + nrm(ks[10], (L, SGU_HEADS, SGU_CHUNK), 0.1),
        "p_a": nrm(ks[11], (L, POOL_WIDTH, D), BETA * POOL_WIDTH ** -0.5),
        "p_b": nrm(ks[12], (L, SGU_WIDTH, D), BETA * SGU_WIDTH ** -0.5),
        "w_out": nrm(ks[13], (L, D, D), BETA * D ** -0.5),
        "ln1_g": 1.0 + nrm(ks[14], (L, D), 0.01),
        "ln1_b": nrm(ks[15], (L, D), 0.01),
        "w_router": nrm(ks[16], (L, D, N_EXPERTS), D ** -0.5),
        "w_gate": nrm(ks[17], (L, N_EXPERTS, D, D_EXPERT), D ** -0.5),
        "w_up": nrm(ks[18], (L, N_EXPERTS, D, D_EXPERT), D ** -0.5),
        "w_down": nrm(ks[19], (L, N_EXPERTS, D_EXPERT, D), BETA * D_EXPERT ** -0.5),
        "ln2_g": 1.0 + nrm(ks[20], (L, D), 0.01),
        "ln2_b": nrm(ks[21], (L, D), 0.01),
    }

def reference(x, in_ln_g, in_ln_b, w_in, b_in, pool_w, pool_scale, sgu_ln_g, sgu_ln_b, sgu_w, sgu_b,
              p_a, p_b, w_out, ln1_g, ln1_b, w_router, w_gate, w_up, w_down, ln2_g, ln2_b):
    h = layer_norm(x, in_ln_g, in_ln_b)
    for l in range(DEPTH):
        mix = hybrid_mixer(h, w_in[l], b_in[l], pool_w[l], pool_scale[l], sgu_ln_g[l], sgu_ln_b[l],
                           sgu_w[l], sgu_b[l], p_a[l], p_b[l], w_out[l])
        h = layer_norm(ALPHA * h + mix, ln1_g[l], ln1_b[l])
        ffn = expert_choice_ffn(h, w_router[l], w_gate[l], w_up[l], w_down[l])
        h = layer_norm(ALPHA * h + ffn, ln2_g[l], ln2_b[l])
    return h


_drawn_inputs = setup_inputs


def setup_inputs(seed=0):
    import zlib

    import numpy as np

    out = dict(_drawn_inputs(seed))
    spreads = {}
    factors = {'in_ln_g': 4.703,
     'in_ln_b': 5.425,
     'b_in': 8.0,
     'pool_scale': 3.679,
     'sgu_ln_g': 8.0,
     'sgu_ln_b': 8.0,
     'sgu_b': 4.91,
     'ln1_g': 5.102,
     'ln1_b': 5.657,
     'ln2_g': 5.907,
     'ln2_b': 5.493}
    for name, (base, spread) in spreads.items():
        noise = np.random.default_rng([zlib.crc32(name.encode()), seed]).standard_normal(out[name].shape)
        drawn = base * np.exp(spread * noise) if base else spread * noise
        out[name] = __import__('jax').numpy.asarray(drawn.astype(out[name].dtype))
    for name, factor in factors.items():
        out[name] = (out[name] * factor).astype(out[name].dtype)
    return out
```

```python
import concourse.bass as bass
from concourse import mybir
from contextlib import ExitStack

FP = mybir.dt.float32
FR = mybir.dt.float32r
U32 = mybir.dt.uint32
ACT = mybir.ActivationFunctionType
ALU = mybir.AluOpType
AX = mybir.AxisListType

P = 128
D = 1024
S = 1024
KT = D // P
MT = S // P
HALF = 512
WINDOWS = (2, 4, 8, 16)
NG = len(WINDOWS)
PW = NG * P
NE = 16
CAP = 2 * S // NE
F = 2 * D
ALPHA = 2.0 ** 0.25
EPS = 1e-5
PAD = 8
PADW = S + 2 * PAD
ROW = D + NE

C_A, C_U, C_V, C_GA, C_GB = 0, PW, PW + D, PW + 2 * D, PW + 3 * D
N_BIN = (PW + 4 * D) // P
COL_SCALE, COL_G, COL_B = N_BIN, N_BIN + NG, N_BIN + NG + KT
N_COLS = N_BIN + NG + 2 * KT

U_A, U_GA = 0, 4
U_PA = U_GA + 8
U_V = U_PA + 4
U_U = U_V + 16
U_GP = U_U + 8
U_WO = U_GP + 16
U_END = U_WO + 16
EU = 24
NRAW = 12
NSPLIT = 3


def hybrid_moe_kernel(nc, x, in_ln_g, in_ln_b, w_in, b_in, pool_w, pool_scale, sgu_ln_g, sgu_ln_b,
                      sgu_w, sgu_b, p_a, p_b, w_out, ln1_g, ln1_b, w_router, w_gate, w_up, w_down,
                      ln2_g, ln2_b, out):
    ctx = ExitStack()
    with ctx:
        base = -(-nc.sbuf_base // 32) * 32
        arena = ctx.enter_context(nc.sbuf_tensor("arena", [P, (nc.sbuf_usable_end - base - 32) // 4], FP))
        R_AM = base
        R_HT = R_AM + 32768
        R_VH = R_HT + 65536
        R_VL = R_VH + 32768
        R_WR = R_VL + 32768
        R_WS = R_WR + 8192
        R_T = R_WS + 16384
        R_EX = R_T + 2 * PADW * 4
        R_SM = R_EX + 12288
        top = [R_SM]

        def at(name, shape, off, dt=FP):
            return nc.alloc_sbuf_tensor_at(name, shape, dt, offset=off)

        def small(name, shape, dt=FP):
            n = 4
            for s in shape[1:]:
                n *= s
            off = top[0]
            top[0] += -(-n // 32) * 32
            assert top[0] <= nc.sbuf_usable_end, top[0]
            return at(name, shape, off, dt)

        def sem(name):
            return ctx.enter_context(nc.semaphore(name))

        am = at("am", [P, KT, S], R_AM)
        hT_hi = at("hT_hi", [P, KT, S], R_HT, FR)
        hT_lo = at("hT_lo", [P, KT, S], R_HT + 32768, FR)
        v_hi = at("v_hi", [P, KT, MT, P], R_VH, FR)
        v_lo = at("v_lo", [P, KT, MT, P], R_VL, FR)
        v_f = at("v_f", [P, KT, MT, P], R_VL)
        yb_hi = at("yb_hi", [P, KT, S], R_VH, FR)
        yb_lo = at("yb_lo", [P, KT, S], R_VL, FR)
        yb_f = at("yb_f", [P, KT, S], R_VL)
        xr = at("xr", [P, MT, D], R_VL)
        ya_hi = at("ya_hi", [P, NG, S], R_VL, FR)
        ya_lo = at("ya_lo", [P, NG, S], R_VL + 16384, FR)
        h1 = at("h1", [P, MT, D], R_VL)
        g0 = at("g0", [P, D], R_VH)
        b0 = at("b0", [P, D], R_VH + 4096)
        ws_raw = at("ws_raw", [P, KT, P], R_VH + 8192)
        sb_row = at("sb_row", [P, KT, P], R_VH + 12288)
        wsT = at("wsT", [P, KT, P], R_VH + 16384)
        ones = at("ones", [P, P], R_VH + 20480)
        vec_rows = at("vec_rows", [N_COLS, P], R_VH + 20992)
        apad = at("apad", [P, NG, PADW], R_VH)
        pa_hi = at("pa_hi", [P, S], R_VH + NG * PADW * 4, FR)
        pa_lo = at("pa_lo", [P, S], R_VH + NG * PADW * 4 + 4096, FR)
        pw_raw = at("pw_raw", [P, NG, P], R_VH + NG * PADW * 4 + 8192)
        pw_hi = at("pw_hi", [P, NG, P], R_VH + NG * PADW * 4 + 10240, FR)
        pw_lo = at("pw_lo", [P, NG, P], R_VH + NG * PADW * 4 + 12288, FR)
        g1 = at("g1", [P, D], R_VH)
        b1 = at("b1", [P, D], R_VH + 4096)
        h1T = at("h1T", [P, 2, KT, P], R_VH + 8192)
        ah = at("ah", [P, 2, D], R_VH + 16384)
        wr = at("wr", [P, 2, 1024], R_WR)
        wh = at("wh", [P, 2, 1024], R_WS, FR)
        wl = at("wl", [P, 2, 1024], R_WS + 8192, FR)
        tt = [at(f"tt{i}", [P, PADW], R_T + i * PADW * 4) for i in range(2)]
        bv = at("bv", [P, D], R_T + PADW * 4)
        rr = at("rr", [P, KT, P], R_EX)
        ws_hi = at("ws_hi", [P, KT, P], R_EX + 4096, FR)
        ws_lo = at("ws_lo", [P, KT, P], R_EX + 8192, FR)
        affT = at("affT", [NE, S], R_EX)
        cs = at("cs", [NE, S], R_EX + 4096)
        sel = at("sel", [NE, S], R_EX + 8192)
        g2 = at("g2", [P, D], R_EX)
        b2 = at("b2", [P, D], R_EX + 4096)
        aff = at("aff", [P, MT, NE], R_EX + 8192)
        raw = at("raw", [P, NRAW, 2048], R_AM)
        eh = [at(f"eh{i}", [P, 2048], R_VH + 16384 * i, FR) for i in range(NSPLIT)]
        el = [at(f"el{i}", [P, 2048], R_VH + 16384 * i + 8192, FR) for i in range(NSPLIT)]
        hidT_hi = at("hidT_hi", [P, F // P, P], R_VL + 16384, FR)
        hidT_lo = at("hidT_lo", [P, F // P, P], R_VL + 24576, FR)
        xeT_hi = at("xeT_hi", [P, KT, P], R_WR, FR)
        xeT_lo = at("xeT_lo", [P, KT, P], R_WR + 4096, FR)
        xe = at("xe", [P, ROW], R_WR + 8192)
        hid = at("hid", [P, 2, HALF], R_WR + 8192 + 4160)
        sil = at("sil", [P, 2, HALF], R_WR + 8192 + 4160 + 4096)
        ye = at("ye", [P, D], R_T)
        csb = at("csb", [P, S], R_T + 4096)
        fin = at("fin", [P, MT, D], R_HT)

        ident = small("ident", [P, P])
        cols = small("cols", [P, N_COLS])
        edge = small("edge", [P, NG, 2 * PAD])
        w_rt = at("w_rt", [P, KT, NE], R_VH + 24576)
        stat = small("stat", [P, 2, 2, 6])
        mean = small("mean", [P, 2, 2])
        veps = small("veps", [P, 2])
        rstd = small("rstd", [P, 2])
        mhalf = small("mhalf", [P, 1])
        nmax = small("nmax", [P, 1])
        esum = small("esum", [P, 1])
        rsum = small("rsum", [P, 1])
        top8 = small("top8", [NE, 8])
        slot_no = small("slot_no", [P, 1])
        idx_f = small("idx_f", [P, 1])
        idx_g = small("idx_g", [P, 1], U32)
        idx_s = small("idx_s", [P, 1], U32)
        gate_g = small("gate_g", [P, 1])
        gate_s = small("gate_s", [P, 1])
        ps = [ctx.enter_context(nc.psum_tensor(f"ps{i}", [P, HALF], FP)) for i in range(8)]

        h0_dram = nc.dram_tensor("h0_rows", (S, D), FP, kind="Internal").ap()
        hx_dram = nc.dram_tensor("h1_rows", (S, ROW), FP, kind="Internal").ap()
        acc_dram = nc.dram_tensor("acc_rows", (S, D), FP, kind="Internal").ap()
        cs_dram = nc.dram_tensor("cs_rows", (NE, S), FP, kind="Internal").ap()

        psum_full = [sem(f"psum_full{i}") for i in range(8)]
        psum_free = [sem(f"psum_free{i}") for i in range(8)]
        x_in = [sem(f"x_in{i}") for i in range(MT)]
        vec_in, ws_in, g0_in, pw_in, bv_in, ln1_in, ln2_in, rt_in = (
            sem(n) for n in ("vec_in", "ws_in", "g0_in", "pw_in", "bv_in", "ln1_in", "ln2_in", "rt_in"))
        h0_in = [sem(f"h0_in{i}") for i in range(MT)]
        fin_in = [sem(f"fin_in{i}") for i in range(MT)]
        w_in_s = [sem(f"w_landed{i}") for i in range(2)]
        w_hi_done, w_lo_done, w_used = sem("w_hi_done"), sem("w_lo_done"), sem("w_used")
        consts, ident_ok = sem("consts"), sem("ident_ok")
        stats_done, rstd_done, norm_done, affine_done = (
            sem(n) for n in ("stats_done", "rstd_done", "norm_done", "affine_done"))
        cols_done, wsT_done, ws_lo_done, rr_done = (sem(n) for n in ("cols_done", "wsT_done", "ws_lo_done", "rr_done"))
        ws_hi_done = sem("ws_hi_done")
        hT_hi_done, hT_lo_done = sem("hT_hi_done"), sem("hT_lo_done")
        pad_done, apad_done = sem("pad_done"), sem("apad_done")
        pw_hi_done, pw_lo_done, pa_f_done, pa_hi_done, pa_lo_done = (
            sem(n) for n in ("pw_hi_done", "pw_lo_done", "pa_f_done", "pa_hi_done", "pa_lo_done"))
        ya_hi_done, ya_lo_done, sig_done, am_done = (sem(n) for n in ("ya_hi_done", "ya_lo_done", "sig_done", "am_done"))
        v_add_done, v_gelu_done, v_hi_done, v_lo_done = (
            sem(n) for n in ("v_add_done", "v_gelu_done", "v_hi_done", "v_lo_done"))
        gu_done, yb_f_done, yb_hi_done, yb_lo_done = (
            sem(n) for n in ("gu_done", "yb_f_done", "yb_hi_done", "yb_lo_done"))
        sgb_done, mg_hi_done, mg_lo_done = sem("sgb_done"), sem("mg_hi_done"), sem("mg_lo_done")
        h0_stored, h1_stored, aff_stored, cs_stored, out_stored = (
            sem(n) for n in ("h0_stored", "h1_stored", "aff_stored", "cs_stored", "out_stored"))
        acc_stored = [sem(f"acc_stored{i}") for i in range(2)]
        ah_done, h1T_done, nmax_done, exp_done, aff_done, affT_done, cs_done = (
            sem(n) for n in ("ah_done", "h1T_done", "nmax_done", "exp_done", "aff_done", "affT_done", "cs_done"))
        raw_in = [sem(f"raw_in{i}") for i in range(NRAW)]
        e_hi_done, e_lo_done, e_used = sem("e_hi_done"), sem("e_lo_done"), sem("e_used")
        e_lo_first = sem("e_lo_first")
        gate_s_done = sem("gate_s_done")
        csb_in, idx_done, idx_s_done, gathered, gate_done, scattered = (
            sem(n) for n in ("csb_in", "idx_done", "idx_s_done", "gathered", "gate_done", "scattered"))
        xe_hi_done, xe_lo_done, sil_done, hid_done, hT2_hi_done, hT2_lo_done, ye_done = (
            sem(n) for n in ("xe_hi_done", "xe_lo_done", "sil_done", "hid_done", "hidT_hi_done", "hidT_lo_done", "ye_done"))
        waits_held = {nc.sync.engine: sem("sp_held"), nc.gpsimd.engine: sem("pool_held")}
        dve_step, pool_step = sem("dve_step"), sem("pool_step")

        order = ["cols", ("ws", 0), ("ws", 1), ("rw", 0), ("rw", 1)]
        order += [("h", m, i) for m in range(MT) for i in range(2)]
        order += [("a", g, i) for g in range(NG) for i in range(2)]
        for n in range(KT):
            order += [("ga", n, i) for i in range(2)]
            if 2 <= n < 2 + NG:
                order += [("ya", n - 2, i) for i in range(2)]
        order += [("pa", n, i) for n in range(KT) for i in range(2)]
        for grp in range(2):
            order += [("v", m, j) for m in range(4 * grp, 4 * grp + 4) for j in range(2)]
        order += [("u", 0, 0), ("u", 0, 1)]
        for h in range(KT):
            if h + 1 < KT:
                order += [("u", h + 1, 0), ("u", h + 1, 1)]
            order += [("mix", h, 0), ("mix", h, 1)]
        for n in range(KT):
            order += [("gb", n, 0), ("gb", n, 1), ("pb", n, 0), ("pb", n, 1)]
        order += [("wo", m, j) for m in range(4) for j in range(2)]
        order += [("wo", m, j) for m in range(4, MT) for j in range(2)]
        for m in range(MT):
            order += [("t", m, 0), ("t", m, 1), ("lg", m), ("at", m)]
        order += [("xt", 0), ("xt", 1)]
        JOB = {name: q for q, name in enumerate(order)}
        Q0 = len(order)
        e_order = [("g", 0), ("u", 0), ("g", 1), ("u", 1), ("t", 0), ("g", 2), ("u", 2), ("t", 1), ("g", 3), ("u", 3),
                   ("t", 2), ("x", 0), ("d", 0), ("d", 1), ("t", 3), ("x", 1)]
        EJOB = {name: Q0 + c for c, name in enumerate(e_order)}

        def bank(name):
            return ps[JOB[name] % 8]

        def wait_full(eng, name):
            q = JOB[name]
            eng.wait_ge(psum_full[q % 8], q // 8 + 1)

        def wait_free(name):
            q = JOB[name]
            if q >= 8:
                nc.tensor.wait_ge(psum_free[q % 8], q // 8)

        def full(name):
            return psum_full[JOB[name] % 8]

        def free(name):
            return psum_free[JOB[name] % 8]

        def ebank(name):
            return ps[EJOB[name] % 8]

        def e_wait_full(eng, name, e):
            q = EJOB[name]
            eng.wait_ge(psum_full[q % 8], q // 8 + 1 + 2 * e)

        def e_wait_free(name, e):
            q = EJOB[name]
            nc.tensor.wait_ge(psum_free[q % 8], q // 8 + 2 * e)

        def e_full(name):
            return psum_full[EJOB[name] % 8]

        def e_free(name):
            return psum_free[EJOB[name] % 8]

        last_job, used_no = {}, {}
        for g in range(NG):
            last_job[U_A + g] = ("a", g, 1)
        for n in range(KT):
            last_job[U_GA + n] = ("ga", n, 1)
            last_job[U_U + n] = ("u", n, 1)
            last_job[U_GP + 2 * n] = ("gb", n, 1)
            last_job[U_GP + 2 * n + 1] = ("pb", n, 1)
        for n in range(4):
            last_job[U_PA + n] = ("pa", 2 * n + 1, 1)
        for grp in range(2):
            last_job[U_V + 8 * grp + 7] = ("v", 4 * grp + 3, 1)
            last_job[U_WO + 8 * grp + 7] = ("wo", 4 * grp + 3, 1)
        for i in range(U_END):
            if i not in last_job:
                used_no[i] = len(used_no) + 1

        def wait_unit_used(eng, i):
            if i in last_job:
                wait_full(eng, last_job[i])
            else:
                eng.wait_ge(w_used, used_no[i])

        def e_wait_used(eng, u, e):
            if u < 16 and u % 2:
                e_wait_full(eng, ("gu"[u // 2 % 2], u // 4), e)
            elif u == EU - 1:
                e_wait_full(eng, ("d", 1), e)
            else:
                eng.wait_ge(e_used, 15 * e + (u // 2 + 1 if u < 16 else u - 7))

        w_in_v = w_in[0].rearrange("(k p) n -> p k n", p=P)
        pa_v = p_a[0].rearrange("(k p) n -> p k n", p=P)
        pb_v = p_b[0].rearrange("(k p) n -> p k n", p=P)

        def unit_source(i):
            if i < U_GA:
                return w_in_v[:, :, C_A + P * i:C_A + P * i + P]
            if i < U_PA:
                return w_in_v[:, :, C_GA + P * (i - U_GA):C_GA + P * (i - U_GA) + P]
            if i < U_V:
                return pa_v[:, :, 2 * P * (i - U_PA):2 * P * (i - U_PA) + 2 * P]
            if i < U_U:
                return w_in_v[:, (i - U_V) % 8, C_V:C_V + D]
            if i < U_GP:
                return w_in_v[:, :, C_U + P * (i - U_U):C_U + P * (i - U_U) + P]
            if i < U_WO:
                n, which = divmod(i - U_GP, 2)
                v = pb_v if which else w_in_v[:, :, C_GB:C_GB + D]
                return v[:, :, P * n:P * n + P]
            k = (i - U_WO) % 8
            return w_out[0, P * k:P * k + P, :]

        def as_source(t, i):
            if U_PA <= i < U_V:
                return t.rearrange("p (k n) -> p k n", n=2 * P)
            if U_V <= i < U_U or i >= U_WO:
                return t
            return t.rearrange("p (k n) -> p k n", n=P)

        wg_v = w_gate[0].rearrange("e (k p) f -> p e k f", p=P)
        wu_v = w_up[0].rearrange("e (k p) f -> p e k f", p=P)
        wd_v = w_down[0].rearrange("e (k p) n -> p e k n", p=P)

        def expert_source(u, e):
            if u < 16:
                j, half = divmod(u, 4)
                v = wu_v if half >= 2 else wg_v
                k = 4 * (half % 2)
                return v[:, bass.ds(e, 1), k:k + 4, HALF * j:HALF * j + HALF].rearrange("p a k f -> p (a k) f")
            k = 2 * (u - 16)
            return wd_v[:, bass.ds(e, 1), k:k + 2, :].rearrange("p a k f -> p (a k) f")

        def held(eng):
            eng.sem_inc(waits_held[eng.engine], 1)

        def flat(t):
            return t.rearrange("p a b -> p (a b)")

        block = ctx.enter_context(nc.Block())

        @block.sync
        def _(sp):
            vec = vec_rows
            sp.dma_start(vec[0:N_BIN, :], b_in[0].rearrange("(c p) -> c p", p=P)).then_inc(vec_in, 16)
            sp.dma_start(vec[COL_SCALE:COL_SCALE + NG, :], pool_scale[0].rearrange("(c p) -> c p", p=P)).then_inc(vec_in, 16)
            sp.dma_start(vec[COL_G:COL_G + KT, :], sgu_ln_g[0].rearrange("(c p) -> c p", p=P)).then_inc(vec_in, 16)
            sp.dma_start(vec[COL_B:COL_B + KT, :], sgu_ln_b[0].rearrange("(c p) -> c p", p=P)).then_inc(vec_in, 16)
            sp.dma_start(xr[:, 0, :], x[0, 0:P, :]).then_inc(x_in[0], 16)
            sp.dma_start(g0[:], in_ln_g.partition_broadcast(P)).then_inc(g0_in, 16)
            sp.dma_start(b0[:], in_ln_b.partition_broadcast(P)).then_inc(g0_in, 16)
            for m in range(1, MT):
                sp.dma_start(xr[:, m, :], x[0, P * m:P * m + P, :]).then_inc(x_in[m], 16)
                if m == 2:
                    sp.dma_start(ws_raw[:], sgu_w[0].rearrange("h p q -> p h q")).then_inc(ws_in, 16)
                    sp.dma_start(sb_row[:].rearrange("p h q -> p (h q)"),
                                 sgu_b[0].rearrange("h p -> (h p)").partition_broadcast(P)).then_inc(ws_in, 16)
            for i in range(U_END):
                if i >= 2:
                    sp.wait_ge(w_lo_done, i - 1)
                sp.dma_start(as_source(wr[:, i % 2, :], i), unit_source(i)).then_inc(w_in_s[i % 2], 16)
                if i == 1:
                    for m in range(MT):
                        sp.wait_ge(affine_done, m + 1)
                        sp.dma_start(h0_dram[P * m:P * m + P, :], xr[:, m, :]).then_inc(h0_stored, 16)
            sp.wait_ge(mg_lo_done, KT)
            for u in range(NRAW):
                if u == 4:
                    wait_full(sp, ("wo", MT - 1, 1))
                sp.dma_start(raw[:, u, :].rearrange("p (k f) -> p k f", k=4), expert_source(u, 0)).then_inc(raw_in[u], 16)
            sp.wait_ge(cs_done, 1)
            sp.dma_start(cs_dram[:, :], cs[:]).then_inc(cs_stored, 16)

            def load(u, e, g):
                sp.wait_ge(e_lo_done, g - NRAW + 1)
                held(sp)
                k = 4 if u < 16 else 2
                sp.dma_start(raw[:, u % NRAW, :].rearrange("p (k f) -> p k f", k=k), expert_source(u, e)).then_inc(raw_in[u % NRAW], 16)

            with sp.Fori(0, NE - 1) as e:
                for u in range(NRAW, EU):
                    load(u, e, EU * e + u)
                for u in range(NRAW):
                    load(u, e + 1, EU * e + EU + u)
            for u in range(NRAW, EU):
                load(u, NE - 1, EU * (NE - 1) + u)

            sp.wait_ge(scattered, 16 * NE)
            for m in range(MT):
                sp.dma_start(fin[:, m, :], acc_dram[P * m:P * m + P, :]).then_inc(fin_in[m], 16)
            for m in range(MT):
                sp.wait_ge(affine_done, 2 * MT + m + 1)
                sp.dma_start(out[0, P * m:P * m + P, :], fin[:, m, :]).then_inc(out_stored, 16)
            sp.wait_ge(out_stored, 16 * MT)

        @block.gpsimd
        def _(pool):
            steps = [0]

            def link(ins):
                steps[0] += 1
                ins.then_inc(pool_step, 1)
                pool.wait_ge(pool_step, steps[0])

            link(nc.gpsimd.memset(ident[:], 0.0))
            nc.gpsimd.affine_select(out=ident[:], in_=ident[:], compare_op=ALU.not_equal, fill=1.0, base=0,
                                    pattern=[[-1, P]], channel_multiplier=1).then_inc(ident_ok, 1)
            nc.gpsimd.memset(mhalf[:], -0.5).then_inc(consts, 1)
            nc.gpsimd.memset(ones[:], 1.0).then_inc(consts, 1)
            nc.gpsimd.iota(slot_no[:], [[0, 1]], base=0, channel_multiplier=1,
                           allow_small_or_imprecise_dtypes=True).then_inc(consts, 1)
            nc.gpsimd.memset(edge[:], 1.0).then_inc(consts, 1)
            pool.wait_ge(consts, 4)
            for g, w in enumerate(WINDOWS):
                for t in range(w // 2):
                    nc.gpsimd.memset(edge[:, g, t:t + 1], w / (t + w // 2)).then_inc(consts, 1)
                for t in range(S - w // 2 + 1, S):
                    nc.gpsimd.memset(edge[:, g, t - S + 2 * PAD:t - S + 2 * PAD + 1], w / (S - t + w // 2)).then_inc(consts, 1)

            def rsqrt(i):
                pool.wait_ge(stats_done, i + 1)
                nc.gpsimd.tensor_tensor(rstd[:, i % 2:i % 2 + 1], veps[:, i % 2:i % 2 + 1], mhalf[:], ALU.pow).then_inc(rstd_done, 1)

            def bias_add(t, b, i):
                pool.wait_ge(norm_done, i + 1)
                nc.gpsimd.tensor_tensor(t, t, b, ALU.add).then_inc(affine_done, 1)

            rsqrt(0)
            pool.wait_ge(g0_in, 32)
            for m in range(MT):
                if m + 1 < MT:
                    rsqrt(m + 1)
                bias_add(xr[:, m, :], b0[:], m)
            pool.wait_ge(hT_lo_done, 2 * MT)
            nc.gpsimd.memset(apad[:, :, 0:PAD], 0.0).then_inc(pad_done, 1)
            nc.gpsimd.memset(apad[:, :, PAD + S:PADW], 0.0).then_inc(pad_done, 1)
            pool.dma_start(pw_raw[:], pool_w[0].rearrange("g c d -> c g d")).then_inc(pw_in, 16)
            pool.wait_ge(pa_lo_done, NG)
            pool.dma_start(bv[:], b_in[0, C_V:C_V + D].partition_broadcast(P)).then_inc(bv_in, 16)
            for m in range(MT):
                rsqrt(MT + m)
            wait_full(pool, ("pb", KT - 1, 1))
            pool.wait_ge(h0_stored, 16 * MT)
            pool.dma_start(g1[:], ln1_g[0].partition_broadcast(P)).then_inc(ln1_in, 16)
            pool.dma_start(b1[:], ln1_b[0].partition_broadcast(P)).then_inc(ln1_in, 16)
            pool.dma_start(w_rt[:], w_router[0].rearrange("(k p) e -> p k e", p=P)).then_inc(rt_in, 16)
            for m in range(MT):
                pool.dma_start(h1[:, m, :], h0_dram[P * m:P * m + P, :]).then_inc(h0_in[m], 16)
            pool.wait_ge(ln1_in, 32)
            for grp in range(2):
                rsqrt(2 * MT + 4 * grp)
                for m in range(4 * grp, 4 * grp + 4):
                    if m % 4 < 3:
                        rsqrt(2 * MT + m + 1)
                    bias_add(h1[:, m, :], b1[:], 2 * MT + m)

            def lo_part(u):
                pool.wait_ge(e_hi_done, u + 1)
                nc.gpsimd.tensor_tensor(el[u][:], raw[:, u, :], eh[u][:].bitcast(FP), ALU.subtract).then_inc(e_lo_first, 1)

            for u in range(NSPLIT):
                lo_part(u)
            pool.wait_ge(h1_stored, 16 * MT)
            pool.wait_ge(aff_stored, 16)
            for i in range(2):
                pool.wait_ge(acc_stored[i], 16 * MT // 2)
            pool.wait_ge(cs_stored, 16)

            def load_counts(e):
                pool.dma_start(csb[:], cs_dram[bass.ds(e, 1), :].rearrange("a s -> (a s)").partition_broadcast(P)).then_inc(csb_in, 16)

            def gather(e):
                pool.wait_ge(idx_done, e + 1)
                held(pool)
                nc.gpsimd.indirect_dma_start(out=xe[:], out_offset=None, in_=hx_dram[:, :],
                                             in_offset=bass.IndirectOffsetOnAxis(ap=idx_g[:], axis=0)).then_inc(gathered, 16)
                pool.wait_ge(gathered, 16 * e + 16)
                nc.gpsimd.tensor_copy(gate_g[:], xe[:, bass.ds(D + e, 1)]).then_inc(gate_done, 1)

            load_counts(0)
            pool.dma_start(g2[:], ln2_g[0].partition_broadcast(P)).then_inc(ln2_in, 16)
            pool.dma_start(b2[:], ln2_b[0].partition_broadcast(P)).then_inc(ln2_in, 16)
            gather(0)

            def body(e, last):
                pool.wait_ge(gate_done, e + 1)
                held(pool)
                nc.gpsimd.tensor_copy(gate_s[:], gate_g[:]).then_inc(gate_s_done, 1)
                nc.gpsimd.tensor_copy(idx_s[:], idx_g[:]).then_inc(idx_s_done, 1)
                if not last:
                    load_counts(e + 1)
                    gather(e + 1)
                pool.wait_ge(ye_done, 2 * e + 2)
                pool.wait_ge(idx_s_done, e + 1)
                held(pool)
                nc.gpsimd.indirect_dma_start(out=acc_dram[:, :], out_offset=bass.IndirectOffsetOnAxis(ap=idx_s[:], axis=0),
                                             in_=ye[:], in_offset=None, compute_op=ALU.add).then_inc(scattered, 16)
                pool.wait_ge(scattered, 16 * e + 16)

            with pool.Fori(0, NE - 1) as e:
                body(e, False)
            body(NE - 1, True)

            pool.wait_ge(ln2_in, 32)
            rsqrt(3 * MT)
            for m in range(MT):
                if m + 1 < MT:
                    rsqrt(3 * MT + m + 1)
                bias_add(fin[:, m, :], b2[:], 3 * MT + m)

        @block.scalar
        def _(act):
            def w_hi(i):
                act.wait_ge(w_in_s[i % 2], 16 * (i // 2 + 1))
                if i >= 2:
                    wait_unit_used(act, i - 2)
                nc.scalar.activation(wh[:, i % 2, :], wr[:, i % 2, :], ACT.Copy).then_inc(w_hi_done, 1)

            wait_full(act, "cols")
            nc.scalar.activation(cols[:], bank("cols")[:, 0:N_COLS], ACT.Copy).then_inc(cols_done, 1)
            act.wait_ge(cols_done, 1)
            act.sem_inc(free("cols"), 1)
            for i in range(2):
                wait_full(act, ("ws", i))
                nc.scalar.activation(flat(wsT[:, 4 * i:4 * i + 4, :]), bank(("ws", i))[:], ACT.Copy).then_inc(wsT_done, 1)
                nc.scalar.activation(flat(ws_hi[:, 4 * i:4 * i + 4, :]), bank(("ws", i))[:], ACT.Copy).then_inc(ws_hi_done, 1)
            w_hi(0)
            w_hi(1)
            for m in range(MT):
                for i in range(2):
                    wait_full(act, ("h", m, i))
                    nc.scalar.activation(hT_hi[:, 4 * i:4 * i + 4, P * m:P * m + P],
                                         bank(("h", m, i))[:].rearrange("p (k t) -> p k t", t=P), ACT.Copy).then_inc(hT_hi_done, 1)

            def a_evac(g):
                for i in range(2):
                    wait_full(act, ("a", g, i))
                    act.wait_ge(pad_done, 2)
                    nc.scalar.activation(apad[:, g, PAD + HALF * i:PAD + HALF * i + HALF], bank(("a", g, i))[:], ACT.Identity,
                                         bias=cols[:, g:g + 1]).then_inc(apad_done, 1)
                    act.wait_ge(apad_done, 2 * g + i + 1)
                    act.sem_inc(free(("a", g, i)), 1)

            def sigmoid_ga(n):
                c = C_GA // P + n
                for i in range(2):
                    wait_full(act, ("ga", n, i))
                    nc.scalar.activation(am[:, n, HALF * i:HALF * i + HALF], bank(("ga", n, i))[:], ACT.Sigmoid,
                                         bias=cols[:, c:c + 1]).then_inc(free(("ga", n, i)), 1)

            def pa_hi_part(g):
                act.wait_ge(pa_f_done, g + 1)
                if g:
                    wait_full(act, ("ya", g - 1, 1))
                nc.scalar.activation(pa_hi[:], tt[0][:, 0:S], ACT.Copy).then_inc(pa_hi_done, 1)

            def ya_hi_part(g):
                for i in range(2):
                    wait_full(act, ("ya", g, i))
                    nc.scalar.activation(ya_hi[:, g, HALF * i:HALF * i + HALF], bank(("ya", g, i))[:], ACT.Copy,
                                         scale=cols[:, COL_SCALE + g:COL_SCALE + g + 1]).then_inc(ya_hi_done, 1)

            for g in range(NG):
                w_hi(U_A + g + 2)
                a_evac(g)
            act.wait_ge(pw_in, 16)
            nc.scalar.activation(pw_hi[:], pw_raw[:], ACT.Copy).then_inc(pw_hi_done, 1)
            for n in range(KT):
                w_hi(U_GA + n + 2)
                sigmoid_ga(n)
                if 2 <= n < 2 + NG:
                    ya_hi_part(n - 2)
                if 1 <= n < 1 + NG:
                    pa_hi_part(n - 1)
            for i in range(U_PA + 2, U_V + 2):
                w_hi(i)

            def gelu_v(m):
                act.wait_ge(v_add_done, 2 * m + 2)
                nc.scalar.activation(v_f[:, :, m, :], v_f[:, :, m, :], ACT.Gelu_apprx_tanh).then_inc(v_gelu_done, 1)

            def v_hi_part(m):
                act.wait_ge(norm_done, MT + m + 1)
                nc.scalar.activation(v_hi[:, :, m, :], v_f[:, :, m, :], ACT.Copy).then_inc(v_hi_done, 1)

            for i in range(U_V + 2, U_V + 10):
                w_hi(i)
            for m in range(4):
                gelu_v(m)
                w_hi(U_V + 10 + m)
            for m in range(4):
                v_hi_part(m)
                if m < 2:
                    w_hi(U_V + 14 + m)
            w_hi(U_U)
            w_hi(U_U + 1)
            for m in range(4, MT):
                gelu_v(m)
            for m in range(4, MT):
                v_hi_part(m)

            def gelu_u(h):
                for i in range(2):
                    wait_full(act, ("u", h, i))
                    if h >= 2:
                        act.wait_ge(yb_f_done, h - 1)
                    nc.scalar.activation(tt[h % 2][:, HALF * i:HALF * i + HALF], bank(("u", h, i))[:], ACT.Gelu_apprx_tanh,
                                         bias=cols[:, C_U // P + h:C_U // P + h + 1]).then_inc(gu_done, 1)
                    act.wait_ge(gu_done, 2 * h + i + 1)
                    act.sem_inc(free(("u", h, i)), 1)

            def yb_hi_part(h):
                act.wait_ge(yb_f_done, h + 1)
                nc.scalar.activation(yb_hi[:, h, :], yb_f[:, h, :], ACT.Copy).then_inc(yb_hi_done, 1)

            gelu_u(0)
            for h in range(KT):
                w_hi(U_U + h + 2)
                if h + 1 < KT:
                    gelu_u(h + 1)
                yb_hi_part(h)

            def sigmoid_gb(n):
                for i in range(2):
                    wait_full(act, ("gb", n, i))
                    if n:
                        act.wait_ge(am_done, 2 * KT + 2 * n - 1 + i)
                    nc.scalar.activation(tt[0][:, HALF * i:HALF * i + HALF], bank(("gb", n, i))[:], ACT.Sigmoid,
                                         bias=cols[:, C_GB // P + n:C_GB // P + n + 1]).then_inc(sgb_done, 1)
                    act.wait_ge(sgb_done, 2 * n + i + 1)
                    act.sem_inc(free(("gb", n, i)), 1)

            def merged_hi(n):
                act.wait_ge(am_done, 2 * KT + 2 * n + 2)
                nc.scalar.activation(hT_hi[:, n, :], am[:, n, :], ACT.Copy).then_inc(mg_hi_done, 1)

            for n in range(KT):
                w_hi(U_GP + 2 * n + 2)
                sigmoid_gb(n)
                if n == KT - 1:
                    for k in range(KT - 1):
                        merged_hi(k)
                w_hi(U_GP + 2 * n + 3)
            merged_hi(KT - 1)

            def row_exp(m):
                act.wait_ge(nmax_done, m + 1)
                nc.scalar.activation(aff[:, m, :], bank(("lg", m))[:, 0:NE], ACT.Exp, bias=nmax[:],
                                     accum_out=esum[:]).then_inc(exp_done, 1)
                act.wait_ge(exp_done, m + 1)
                act.sem_inc(free(("lg", m)), 1)

            def row_out(m):
                act.wait_ge(affine_done, MT + m + 1)
                if m >= 2:
                    act.wait_ge(acc_stored[m % 2], 16 * (m // 2))
                nc.scalar.activation(ah[:, m % 2, :], h1[:, m, :], ACT.Copy, scale=ALPHA).then_inc(ah_done, 1)
                act.dma_start(hx_dram[P * m:P * m + P, 0:D], h1[:, m, :]).then_inc(h1_stored, 16)
                act.wait_ge(ah_done, m + 1)
                act.dma_start(acc_dram[P * m:P * m + P, :], ah[:, m % 2, :]).then_inc(acc_stored[m % 2], 16)

            def route_1(m):
                for i in range(2):
                    wait_full(act, ("t", m, i))
                    nc.scalar.activation(flat(h1T[:, m % 2, 4 * i:4 * i + 4, :]), bank(("t", m, i))[:], ACT.Copy).then_inc(h1T_done, 1)
                    act.wait_ge(h1T_done, 2 * m + i + 1)
                    act.sem_inc(free(("t", m, i)), 1)

            def route_2(m):
                wait_full(act, ("at", m))
                nc.scalar.activation(affT[:, P * m:P * m + P], bank(("at", m))[0:NE, 0:P], ACT.Copy).then_inc(affT_done, 1)
                act.wait_ge(affT_done, m + 1)
                act.sem_inc(free(("at", m)), 1)

            for i in range(U_WO + 2, U_WO + 10):
                w_hi(i)
            for m in range(4):
                w_hi(U_WO + 10 + m)
                row_out(m)
            for i in range(U_WO + 14, U_WO + 16):
                w_hi(i)
            for m in range(MT):
                if m >= 4:
                    row_out(m)
                route_1(m)
                row_exp(m)
                route_2(m)
            act.wait_ge(aff_done, MT)
            act.dma_start(hx_dram[:, D:ROW].rearrange("(m p) e -> p m e", p=P), aff[:]).then_inc(aff_stored, 16)

            def e_hi(u, s, g, e_cur, wait_used=True):
                act.wait_ge(raw_in[u % NRAW], s + 16)
                if wait_used:
                    prev = u - NSPLIT
                    e_wait_used(act, prev % EU, e_cur if prev >= 0 else e_cur - 1)
                nc.scalar.activation(eh[u % NSPLIT][:], raw[:, u % NRAW, :], ACT.Copy).then_inc(e_hi_done, 1)

            for i in range(2):
                act.wait_ge(acc_stored[i], 16 * MT // 2)
            act.wait_ge(h1_stored, 16 * MT)
            for u in range(NSPLIT):
                e_hi(u, 0, u, 0, wait_used=False)

            def x_hi(src, i, waiter):
                waiter()
                nc.scalar.activation(flat(xeT_hi[:, 4 * i:4 * i + 4, :]), src, ACT.Copy).then_inc(xe_hi_done, 1)

            for i in range(2):
                x_hi(bank(("xt", i))[:], i, lambda: wait_full(act, ("xt", i)))

            def silu(j, e):
                e_wait_full(act, ("g", j), e)
                nc.scalar.activation(sil[:, j % 2, :], ebank(("g", j))[:], ACT.Silu).then_inc(sil_done, 1)
                act.wait_ge(sil_done, 4 * e + j + 1)
                act.sem_inc(e_free(("g", j)), 1)

            def hidT_hi_part(j, e):
                e_wait_full(act, ("t", j), e)
                nc.scalar.activation(flat(hidT_hi[:, 4 * j:4 * j + 4, :]), ebank(("t", j))[:], ACT.Copy).then_inc(hT2_hi_done, 1)

            def body(e, last):
                for u in range(NSPLIT, EU):
                    e_hi(u, 32 * e + 16 * (u // NRAW), EU * e + u, e)
                    if u in (6, 10, 14):
                        silu((u - 6) // 4, e)
                    if u in (10, 14, 18, 21):
                        hidT_hi_part((10, 14, 18, 21).index(u), e)
                    if u == 18:
                        silu(3, e)
                    if not last and u in (18, 21):
                        i = (18, 21).index(u)
                        x_hi(ebank(("x", i))[:], i, lambda: e_wait_full(act, ("x", i), e))
                if not last:
                    for u in range(NSPLIT):
                        e_hi(u, 32 * (e + 1), EU * e + EU + u, e + 1)
                act.wait_ge(idx_s_done, e + 1)
                act.wait_ge(gate_s_done, e + 1)
                for i in range(2):
                    e_wait_full(act, ("d", i), e)
                    nc.scalar.activation(ye[:, HALF * i:HALF * i + HALF], ebank(("d", i))[:], ACT.Copy,
                                         scale=gate_s[:]).then_inc(ye_done, 1)
                act.wait_ge(ye_done, 2 * e + 2)
                act.sem_inc(e_free(("d", 0)), 1)
                act.sem_inc(e_free(("d", 1)), 1)

            with act.Fori(0, NE - 1) as e:
                body(e, False)
            body(NE - 1, True)

        @block.vector
        def _(dve):
            steps = [0]

            def link(ins):
                steps[0] += 1
                ins.then_inc(dve_step, 1)
                dve.wait_ge(dve_step, steps[0])

            def w_lo(i):
                dve.wait_ge(w_hi_done, i + 1)
                nc.vector.tensor_tensor(wl[:, i % 2, :], wr[:, i % 2, :], wh[:, i % 2, :].bitcast(FP), ALU.subtract).then_inc(w_lo_done, 1)

            def stats(lo_half, hi_half, i):
                s = i % 2
                nc.vector.bn_stats(stat[:, s, 0, :], lo_half)
                link(nc.vector.bn_stats(stat[:, s, 1, :], hi_half))
                link(nc.vector.bn_aggr(mean[:, s, :], stat[:, s, :, :]))
                nc.vector.tensor_scalar(veps[:, s:s + 1], mean[:, s, 1:2], EPS, None, ALU.add).then_inc(stats_done, 1)

            def center(t, i):
                s = i % 2
                dve.wait_ge(rstd_done, i + 1)
                return nc.vector.tensor_scalar(t, t, mean[:, s, 0:1], rstd[:, s:s + 1], ALU.subtract, ALU.mult)

            dve.wait_ge(x_in[0], 16)
            stats(xr[:, 0, 0:HALF], xr[:, 0, HALF:D], 0)
            dve.wait_ge(g0_in, 32)

            def hT_lo_part(m):
                for i in range(2):
                    dve.wait_ge(hT_hi_done, 2 * m + i + 1)
                    nc.vector.tensor_tensor(hT_lo[:, 4 * i:4 * i + 4, P * m:P * m + P],
                                            bank(("h", m, i))[:].rearrange("p (k t) -> p k t", t=P),
                                            hT_hi[:, 4 * i:4 * i + 4, P * m:P * m + P].bitcast(FP),
                                            ALU.subtract).then_inc(hT_lo_done, 1)
                    dve.wait_ge(hT_lo_done, 2 * m + i + 1)
                    dve.sem_inc(free(("h", m, i)), 1)

            for m in range(MT):
                if m + 1 < MT:
                    dve.wait_ge(x_in[m + 1], 16)
                    stats(xr[:, m + 1, 0:HALF], xr[:, m + 1, HALF:D], m + 1)
                link(center(xr[:, m, :], m))
                nc.vector.tensor_tensor(xr[:, m, :], xr[:, m, :], g0[:], ALU.mult).then_inc(norm_done, 1)
                if m == 0:
                    for i in range(2):
                        dve.wait_ge(ws_hi_done, i + 1)
                        nc.vector.tensor_tensor(flat(ws_lo[:, 4 * i:4 * i + 4, :]), bank(("ws", i))[:],
                                                flat(ws_hi[:, 4 * i:4 * i + 4, :]).bitcast(FP), ALU.subtract).then_inc(ws_lo_done, 1)
                        dve.wait_ge(ws_lo_done, i + 1)
                        dve.sem_inc(free(("ws", i)), 1)
                    dve.wait_ge(ws_in, 32)
                    dve.wait_ge(cols_done, 1)
                    for h in range(KT):
                        wait_full(dve, ("rw", h // 4))
                        nc.vector.scalar_tensor_tensor(out=rr[:, h, :], in0=bank(("rw", h // 4))[:, P * (h % 4):P * (h % 4) + P],
                                                       scalar=cols[:, COL_B + h:COL_B + h + 1], in1=sb_row[:, h, :],
                                                       op0=ALU.mult, op1=ALU.add).then_inc(rr_done, 1)
                        if h % 4 == 3:
                            dve.wait_ge(rr_done, h + 1)
                            dve.sem_inc(free(("rw", h // 4)), 1)
                    w_lo(0)
                    w_lo(1)
                if m >= 1:
                    hT_lo_part(m - 1)
            hT_lo_part(MT - 1)

            def pool_group(g):
                w = WINDOWS[g]
                dve.wait_ge(apad_done, 2 * g + 2)
                if g:
                    dve.wait_ge(pa_hi_done, g)
                    dve.wait_ge(pa_lo_done, g)
                src, n, width, step = apad[:, g, :], PADW, 1, 0
                side = 0 if (g + 1) % 2 else 1
                while width < w:
                    n -= width
                    dst = tt[side]
                    if 2 * width == w:
                        s0 = PAD - w // 2
                        link(nc.vector.tensor_tensor(dst[:, 0:S], src[:, s0:s0 + S], src[:, s0 + width:s0 + width + S], ALU.add))
                    else:
                        link(nc.vector.tensor_tensor(dst[:, 0:n], src[:, 0:n], src[:, width:width + n], ALU.add))
                    src = dst
                    side ^= 1
                    width *= 2
                assert src is tt[0]
                for a, b, c in ((0, PAD, 0), (S - PAD, S, PAD)):
                    ins = nc.vector.tensor_tensor(tt[0][:, a:b], tt[0][:, a:b], edge[:, g, c:c + PAD], ALU.mult)
                    link(ins)
                nc.vector.scalar_tensor_tensor(out=tt[0][:, 0:S], in0=tt[0][:, 0:S], scalar=1.0 / w,
                                               in1=apad[:, g, PAD:PAD + S], op0=ALU.mult, op1=ALU.subtract).then_inc(pa_f_done, 1)

            def pa_lo_part(g):
                dve.wait_ge(pa_hi_done, g + 1)
                dve.wait_ge(pa_f_done, g + 1)
                nc.vector.tensor_tensor(pa_lo[:], tt[0][:, 0:S], pa_hi[:].bitcast(FP), ALU.subtract).then_inc(pa_lo_done, 1)

            def ya_lo_part(g):
                for i in range(2):
                    dve.wait_ge(ya_hi_done, 2 * g + i + 1)
                    nc.vector.scalar_tensor_tensor(out=ya_lo[:, g, HALF * i:HALF * i + HALF], in0=bank(("ya", g, i))[:],
                                                   scalar=cols[:, COL_SCALE + g:COL_SCALE + g + 1],
                                                   in1=ya_hi[:, g, HALF * i:HALF * i + HALF].bitcast(FP),
                                                   op0=ALU.mult, op1=ALU.subtract).then_inc(ya_lo_done, 1)
                    dve.wait_ge(ya_lo_done, 2 * g + i + 1)
                    dve.sem_inc(free(("ya", g, i)), 1)

            for g in range(NG):
                w_lo(U_A + g + 2)
            dve.wait_ge(consts, 4 + sum(w - 1 for w in WINDOWS))
            dve.wait_ge(pw_hi_done, 1)
            nc.vector.tensor_tensor(pw_lo[:], pw_raw[:], pw_hi[:].bitcast(FP), ALU.subtract).then_inc(pw_lo_done, 1)
            for n in range(KT):
                w_lo(U_GA + n + 2)
                if 1 <= n < 1 + NG:
                    pa_lo_part(n - 1)
                if n < NG:
                    pool_group(n)
                if 2 <= n < 2 + NG:
                    ya_lo_part(n - 2)

            def pa_merge(n):
                for i in range(2):
                    wait_full(dve, ("pa", n, i))
                    s = slice(HALF * i, HALF * i + HALF)
                    nc.vector.tensor_tensor(am[:, n, s], am[:, n, s], bank(("pa", n, i))[:], ALU.mult).then_inc(am_done, 1)
                    dve.wait_ge(am_done, 2 * n + i + 1)
                    dve.sem_inc(free(("pa", n, i)), 1)

            for i in range(4):
                w_lo(U_PA + i + 2)
                for ct in range(2):
                    pa_merge(2 * i + ct)

            def v_add(m):
                for j in range(2):
                    wait_full(dve, ("v", m, j))
                    dve.wait_ge(bv_in, 16)
                    nc.vector.tensor_tensor(v_f[:, 4 * j:4 * j + 4, m, :], bank(("v", m, j))[:].rearrange("p (h d) -> p h d", d=P),
                                            bv[:, HALF * j:HALF * j + HALF].rearrange("p (h d) -> p h d", d=P), ALU.add).then_inc(v_add_done, 1)
                    dve.wait_ge(v_add_done, 2 * m + j + 1)
                    dve.sem_inc(free(("v", m, j)), 1)

            def v_stats(m):
                dve.wait_ge(v_gelu_done, m + 1)
                stats(v_f[:, 0:4, m, :], v_f[:, 4:8, m, :], MT + m)

            def v_center(m):
                center(v_f[:, :, m, :], MT + m).then_inc(norm_done, 1)

            def v_lo_part(m):
                dve.wait_ge(v_hi_done, m + 1)
                nc.vector.tensor_tensor(v_lo[:, :, m, :], v_f[:, :, m, :], v_hi[:, :, m, :].bitcast(FP), ALU.subtract).then_inc(v_lo_done, 1)

            for i in range(U_V + 2, U_V + 9):
                w_lo(i)
            for m in range(4):
                v_add(m)
            w_lo(U_V + 9)
            v_stats(0)
            for m in range(4):
                if m < 3:
                    v_stats(m + 1)
                w_lo(U_V + 10 + m)
                v_center(m)
                if m:
                    v_lo_part(m - 1)
            v_lo_part(3)
            for i in range(U_V + 14, U_V + 17):
                w_lo(i)
            for m in range(4, MT):
                v_add(m)
            w_lo(U_U + 1)
            v_stats(4)
            for m in range(4, MT):
                if m < MT - 1:
                    v_stats(m + 1)
                v_center(m)
                if m > 4:
                    v_lo_part(m - 1)
            v_lo_part(MT - 1)

            def gate_head(h):
                for i in range(2):
                    wait_full(dve, ("mix", h, i))
                    s = slice(HALF * i, HALF * i + HALF)
                    link(nc.vector.scalar_tensor_tensor(
                        out=yb_f[:, h, s].rearrange("p (c t) -> p c t", t=P), in0=bank(("mix", h, i))[:].rearrange("p (c t) -> p c t", t=P),
                        scalar=cols[:, COL_G + h:COL_G + h + 1], in1=rr[:, h, :].unsqueeze(1).broadcast_to([P, 4, P]),
                        op0=ALU.mult, op1=ALU.add))
                    dve.sem_inc(free(("mix", h, i)), 1)
                dve.wait_ge(gu_done, 2 * h + 2)
                nc.vector.tensor_tensor(yb_f[:, h, :], yb_f[:, h, :], tt[h % 2][:, 0:S], ALU.mult).then_inc(yb_f_done, 1)

            def yb_lo_part(h):
                dve.wait_ge(yb_hi_done, h + 1)
                nc.vector.tensor_tensor(yb_lo[:, h, :], yb_f[:, h, :], yb_hi[:, h, :].bitcast(FP), ALU.subtract).then_inc(yb_lo_done, 1)

            for h in range(KT):
                w_lo(U_U + h + 2)
                gate_head(h)
                if h:
                    yb_lo_part(h - 1)
            yb_lo_part(KT - 1)

            def pb_merge(n):
                for i in range(2):
                    s = slice(HALF * i, HALF * i + HALF)
                    dve.wait_ge(sgb_done, 2 * n + i + 1)
                    wait_full(dve, ("pb", n, i))
                    link(nc.vector.tensor_tensor(tt[1][:, s], tt[0][:, s], bank(("pb", n, i))[:], ALU.mult))
                    dve.sem_inc(free(("pb", n, i)), 1)
                    nc.vector.tensor_tensor(am[:, n, s], am[:, n, s], tt[1][:, s], ALU.add).then_inc(am_done, 1)

            def merged_lo(n):
                dve.wait_ge(mg_hi_done, n + 1)
                nc.vector.tensor_tensor(hT_lo[:, n, :], am[:, n, :], hT_hi[:, n, :].bitcast(FP), ALU.subtract).then_inc(mg_lo_done, 1)

            for n in range(KT):
                w_lo(U_GP + 2 * n + 2)
                if n == KT - 1:
                    for k in range(KT - 1):
                        merged_lo(k)
                w_lo(U_GP + 2 * n + 3) if n < KT - 1 else None
                pb_merge(n)
            w_lo(U_GP + 2 * KT + 1)
            merged_lo(KT - 1)

            def residual(m):
                for j in range(2):
                    s = slice(HALF * j, HALF * j + HALF)
                    dve.wait_ge(h0_in[m], 16)
                    wait_full(dve, ("wo", m, j))
                    link(nc.vector.scalar_tensor_tensor(out=h1[:, m, s], in0=h1[:, m, s], scalar=ALPHA, in1=bank(("wo", m, j))[:],
                                                        op0=ALU.mult, op1=ALU.add))
                    dve.sem_inc(free(("wo", m, j)), 1)

            def h1_scale(m):
                link(center(h1[:, m, :], 2 * MT + m))
                nc.vector.tensor_tensor(h1[:, m, :], h1[:, m, :], g1[:], ALU.mult).then_inc(norm_done, 1)

            def h1_stats(m):
                stats(h1[:, m, 0:HALF], h1[:, m, HALF:D], 2 * MT + m)

            def softmax(m):
                wait_full(dve, ("lg", m))
                nc.vector.tensor_reduce(out=nmax[:], in_=bank(("lg", m))[:, 0:NE], axis=AX.X, op=ALU.max, negate=True).then_inc(nmax_done, 1)
                dve.wait_ge(exp_done, m + 1)
                link(nc.vector.reciprocal(rsum[:], esum[:]))
                nc.vector.tensor_scalar(aff[:, m, :], aff[:, m, :], rsum[:], None, ALU.mult).then_inc(aff_done, 1)

            for i in range(U_WO + 2, U_WO + 9):
                w_lo(i)
            for m in range(4):
                residual(m)
            w_lo(U_WO + 9)
            dve.wait_ge(ln1_in, 32)
            h1_stats(0)
            for m in range(4):
                if m < 3:
                    h1_stats(m + 1)
                w_lo(U_WO + 10 + m)
                h1_scale(m)
            for i in range(U_WO + 14, U_WO + 16):
                w_lo(i)
            for m in range(4, MT):
                residual(m)
            h1_stats(4)
            for m in range(4, MT):
                if m < MT - 1:
                    h1_stats(m + 1)
                h1_scale(m)
                softmax(m - 4)
            for m in range(4, MT):
                softmax(m)

            dve.wait_ge(affT_done, MT)
            for r in range(CAP // 8):
                link(nc.vector.max(top8[:], affT[:]))
                link(nc.vector.match_replace(affT[:], top8[:], affT[:], -1.0))
            dve.wait_ge(aff_stored, 16)
            link(nc.vector.tensor_scalar(sel[:], affT[:], 0.0, None, ALU.is_lt))
            nc.vector.tensor_tensor_scan(cs[:], sel[:], sel[:], 0.0, ALU.add, ALU.max).then_inc(cs_done, 1)

            dve.wait_ge(e_lo_first, NSPLIT)
            dve.sem_inc(e_lo_done, NSPLIT)

            def token_numbers(e):
                dve.wait_ge(csb_in, 16 * e + 16)
                nc.vector.tensor_scalar(csb[:], csb[:], slot_no[:], 0.0, ALU.is_le, ALU.add, accum_out=idx_f[:]).then_inc(dve_step, 1)

            token_numbers(0)
            steps[0] += 1
            dve.wait_ge(dve_step, steps[0])
            nc.vector.tensor_copy(idx_g[:], idx_f[:]).then_inc(idx_done, 1)

            def x_lo(src, i, n):
                dve.wait_ge(xe_hi_done, n)
                nc.vector.tensor_tensor(flat(xeT_lo[:, 4 * i:4 * i + 4, :]), src, flat(xeT_hi[:, 4 * i:4 * i + 4, :]).bitcast(FP),
                                        ALU.subtract).then_inc(xe_lo_done, 1)
                dve.wait_ge(xe_lo_done, n)

            for i in range(2):
                x_lo(bank(("xt", i))[:], i, i + 1)
                dve.sem_inc(free(("xt", i)), 1)

            def e_lo(u, g):
                dve.wait_ge(e_hi_done, g + 1)
                nc.vector.tensor_tensor(el[u % NSPLIT][:], raw[:, u % NRAW, :], eh[u % NSPLIT][:].bitcast(FP), ALU.subtract).then_inc(e_lo_done, 1)

            def hid_part(j, e):
                dve.wait_ge(sil_done, 4 * e + j + 1)
                e_wait_full(dve, ("u", j), e)
                nc.vector.tensor_tensor(hid[:, j % 2, :], sil[:, j % 2, :], ebank(("u", j))[:], ALU.mult).then_inc(hid_done, 1)
                dve.wait_ge(hid_done, 4 * e + j + 1)
                dve.sem_inc(e_free(("u", j)), 1)

            def hidT_lo_part(j, e):
                dve.wait_ge(hT2_hi_done, 4 * e + j + 1)
                nc.vector.tensor_tensor(flat(hidT_lo[:, 4 * j:4 * j + 4, :]), ebank(("t", j))[:],
                                        flat(hidT_hi[:, 4 * j:4 * j + 4, :]).bitcast(FP), ALU.subtract).then_inc(hT2_lo_done, 1)
                dve.wait_ge(hT2_lo_done, 4 * e + j + 1)
                dve.sem_inc(e_free(("t", j)), 1)

            base_steps = steps[0]

            def body(e, last):
                for u in range(NSPLIT, EU):
                    e_lo(u, EU * e + u)
                    if u in (6, 10, 14):
                        hid_part((u - 6) // 4, e)
                    if u in (10, 14, 18, 21):
                        hidT_lo_part((10, 14, 18, 21).index(u), e)
                    if u == 18:
                        hid_part(3, e)
                    if not last and u in (18, 21):
                        i = (18, 21).index(u)
                        x_lo(ebank(("x", i))[:], i, 2 * e + 3 + i)
                        dve.sem_inc(e_free(("x", i)), 1)
                    if not last and u == 8:
                        token_numbers(e + 1)
                        dve.wait_ge(dve_step, base_steps + e + 1)
                        dve.wait_ge(idx_s_done, e + 1)
                        nc.vector.tensor_copy(idx_g[:], idx_f[:]).then_inc(idx_done, 1)
                if not last:
                    for u in range(NSPLIT):
                        e_lo(u, EU * e + EU + u)

            with dve.Fori(0, NE - 1) as e:
                body(e, False)
            body(NE - 1, True)
            steps[0] += NE - 1

            dve.wait_ge(fin_in[0], 16)
            stats(fin[:, 0, 0:HALF], fin[:, 0, HALF:D], 3 * MT)
            dve.wait_ge(ln2_in, 32)
            for m in range(MT):
                if m + 1 < MT:
                    dve.wait_ge(fin_in[m + 1], 16)
                    stats(fin[:, m + 1, 0:HALF], fin[:, m + 1, HALF:D], 3 * MT + m + 1)
                link(center(fin[:, m, :], 3 * MT + m))
                nc.vector.tensor_tensor(fin[:, m, :], fin[:, m, :], g2[:], ALU.mult).then_inc(norm_done, 1)

        @block.tensor
        def _(pe):
            def three(dst, a_hi, a_lo, b_hi, b_lo, start, stop):
                nc.tensor.matmul(dst, a_hi, b_hi, start=start, stop=False)
                nc.tensor.matmul(dst, a_hi, b_lo, start=False, stop=False)
                return nc.tensor.matmul(dst, a_lo, b_hi, start=False, stop=stop)

            pe.wait_ge(ident_ok, 1)
            pe.wait_ge(vec_in, 64)
            nc.tensor.transpose(bank("cols")[:, 0:N_COLS], vec_rows[:], ident[0:N_COLS, 0:N_COLS]).then_inc(full("cols"), 1)
            pe.wait_ge(ws_in, 32)
            for i in range(2):
                for h in range(4):
                    last = nc.tensor.transpose(bank(("ws", i))[:, P * h:P * h + P], ws_raw[:, 4 * i + h, :], ident[:])
                last.then_inc(full(("ws", i)), 1)
            pe.wait_ge(consts, 2)
            for i in range(2):
                pe.wait_ge(wsT_done, i + 1)
                nc.tensor.matmul(bank(("rw", i))[:], ones[:], flat(wsT[:, 4 * i:4 * i + 4, :]), start=True, stop=True).then_inc(full(("rw", i)), 1)
            for m in range(MT):
                pe.wait_ge(affine_done, m + 1)
                for i in range(2):
                    wait_free(("h", m, i))
                    for k in range(4):
                        kk = 4 * i + k
                        last = nc.tensor.transpose(bank(("h", m, i))[:, P * k:P * k + P], xr[:, m, P * kk:P * kk + P], ident[:])
                    last.then_inc(full(("h", m, i)), 1)
            pe.wait_ge(hT_lo_done, 2 * MT)

            def project(i, name, n, a_kts, b_hi, b_lo, off=0, width=P):
                h3 = wh[:, i % 2, :].rearrange("p (k n) -> p k n", n=width)
                l3 = wl[:, i % 2, :].rearrange("p (k n) -> p k n", n=width)
                for half in range(2):
                    wait_free((name, n, half))
                    for k in range(a_kts):
                        last = three(bank((name, n, half))[:], h3[:, k, off:off + P], l3[:, k, off:off + P],
                                     b_hi[:, k, HALF * half:HALF * half + HALF], b_lo[:, k, HALF * half:HALF * half + HALF],
                                     k == 0, k == a_kts - 1)
                    last.then_inc(full((name, n, half)), 1)

            def rows(i, name, ms, k, a_hi, a_lo):
                for m in ms:
                    for j in range(2):
                        if k == 0:
                            wait_free((name, m, j))
                        s = slice(HALF * j, HALF * j + HALF)
                        last = three(bank((name, m, j))[:], a_hi[:, k, P * m:P * m + P], a_lo[:, k, P * m:P * m + P],
                                     wh[:, i % 2, s], wl[:, i % 2, s], k == 0, k == KT - 1)
                        if k == KT - 1:
                            last.then_inc(full((name, m, j)), 1)
                if k < KT - 1:
                    last.then_inc(w_used, 1)

            for g in range(NG):
                pe.wait_ge(w_lo_done, U_A + g + 1)
                project(U_A + g, "a", g, KT, hT_hi, hT_lo)
            for n in range(KT):
                pe.wait_ge(w_lo_done, U_GA + n + 1)
                project(U_GA + n, "ga", n, KT, hT_hi, hT_lo)
                if 2 <= n < 2 + NG:
                    g = n - 2
                    pe.wait_ge(pw_lo_done, 1)
                    pe.wait_ge(pa_lo_done, g + 1)
                    for i in range(2):
                        wait_free(("ya", g, i))
                        s = slice(HALF * i, HALF * i + HALF)
                        three(bank(("ya", g, i))[:], pw_hi[:, g, :], pw_lo[:, g, :], pa_hi[:, s], pa_lo[:, s],
                              True, True).then_inc(full(("ya", g, i)), 1)
            pe.wait_ge(ya_lo_done, 2 * NG)
            for n in range(KT):
                i = U_PA + n // 2
                pe.wait_ge(w_lo_done, i + 1)
                project(i, "pa", n, NG, ya_hi, ya_lo, off=P * (n % 2), width=2 * P)
            for grp in range(2):
                for k in range(KT):
                    i = U_V + 8 * grp + k
                    pe.wait_ge(w_lo_done, i + 1)
                    rows(i, "v", range(4 * grp, 4 * grp + 4), k, hT_hi, hT_lo)

            def u_head(h):
                pe.wait_ge(w_lo_done, U_U + h + 1)
                project(U_U + h, "u", h, KT, hT_hi, hT_lo)

            u_head(0)
            for h in range(KT):
                if h + 1 < KT:
                    u_head(h + 1)
                pe.wait_ge(v_lo_done, MT)
                for i in range(2):
                    wait_free(("mix", h, i))
                    for c in range(4):
                        m = 4 * i + c
                        last = three(bank(("mix", h, i))[:, P * c:P * c + P], v_hi[:, h, m, :], v_lo[:, h, m, :],
                                     ws_hi[:, h, :], ws_lo[:, h, :], True, True)
                    last.then_inc(full(("mix", h, i)), 1)
            for n in range(KT):
                pe.wait_ge(w_lo_done, U_GP + 2 * n + 1)
                project(U_GP + 2 * n, "gb", n, KT, hT_hi, hT_lo)
                if n == 0:
                    pe.wait_ge(yb_lo_done, KT)
                pe.wait_ge(w_lo_done, U_GP + 2 * n + 2)
                project(U_GP + 2 * n + 1, "pb", n, KT, yb_hi, yb_lo)
            for grp in range(2):
                for k in range(KT):
                    i = U_WO + 8 * grp + k
                    pe.wait_ge(w_lo_done, i + 1)
                    pe.wait_ge(mg_lo_done, k + 1)
                    rows(i, "wo", range(4 * grp, 4 * grp + 4), k, hT_hi, hT_lo)

            pe.wait_ge(rt_in, 16)
            for m in range(MT):
                pe.wait_ge(affine_done, MT + m + 1)
                for i in range(2):
                    wait_free(("t", m, i))
                    for k in range(4):
                        kk = 4 * i + k
                        last = nc.tensor.transpose(bank(("t", m, i))[:, P * k:P * k + P], h1[:, m, P * kk:P * kk + P], ident[:])
                    last.then_inc(full(("t", m, i)), 1)
                pe.wait_ge(h1T_done, 2 * m + 2)
                wait_free(("lg", m))
                for k in range(KT):
                    last = nc.tensor.matmul(bank(("lg", m))[:, 0:NE], h1T[:, m % 2, k, :], w_rt[:, k, :], start=(k == 0), stop=(k == KT - 1))
                last.then_inc(full(("lg", m)), 1)
                pe.wait_ge(aff_done, m + 1)
                wait_free(("at", m))
                nc.tensor.transpose(bank(("at", m))[0:NE, 0:P], aff[:, m, :], ident[:]).then_inc(full(("at", m)), 1)

            pe.wait_ge(gathered, 16)
            for i in range(2):
                wait_free(("xt", i))
                for k in range(4):
                    kk = 4 * i + k
                    last = nc.tensor.transpose(bank(("xt", i))[:, P * k:P * k + P], xe[:, P * kk:P * kk + P], ident[:])
                last.then_inc(full(("xt", i)), 1)

            def gate_up(j, e):
                for half in range(4):
                    u = 4 * j + half
                    name = ("gu"[half // 2], j)
                    pe.wait_ge(e_lo_done, EU * e + u + 1)
                    if half % 2 == 0:
                        e_wait_free(name, e)
                    h3 = eh[u % NSPLIT][:].rearrange("p (k f) -> p k f", k=4)
                    l3 = el[u % NSPLIT][:].rearrange("p (k f) -> p k f", k=4)
                    for k in range(4):
                        kk = 4 * (half % 2) + k
                        last = three(ebank(name)[:], xeT_hi[:, kk, :], xeT_lo[:, kk, :], h3[:, k, :], l3[:, k, :], kk == 0, kk == KT - 1)
                    last.then_inc(e_used if half % 2 == 0 else e_full(name), 1)

            def hid_transpose(j, e):
                pe.wait_ge(hid_done, 4 * e + j + 1)
                e_wait_free(("t", j), e)
                for k in range(4):
                    last = nc.tensor.transpose(ebank(("t", j))[:, P * k:P * k + P], hid[:, j % 2, P * k:P * k + P], ident[:])
                last.then_inc(e_full(("t", j)), 1)

            def next_tokens(i, e):
                pe.wait_ge(gathered, 16 * e + 32)
                e_wait_free(("x", i), e)
                for k in range(4):
                    kk = 4 * i + k
                    last = nc.tensor.transpose(ebank(("x", i))[:, P * k:P * k + P], xe[:, P * kk:P * kk + P], ident[:])
                last.then_inc(e_full(("x", i)), 1)

            def down(u, e):
                pe.wait_ge(e_lo_done, EU * e + u + 1)
                h3 = eh[u % NSPLIT][:].rearrange("p (k n) -> p k n", k=2)
                l3 = el[u % NSPLIT][:].rearrange("p (k n) -> p k n", k=2)
                for k in range(2):
                    kk = 2 * (u - 16) + k
                    for j in range(2):
                        s = slice(HALF * j, HALF * j + HALF)
                        last = three(ebank(("d", j))[:], hidT_hi[:, kk, :], hidT_lo[:, kk, :], h3[:, k, s], l3[:, k, s],
                                     kk == 0, kk == F // P - 1)
                        if u == EU - 1 and k == 1:
                            last.then_inc(e_full(("d", j)), 1)
                if u < EU - 1:
                    last.then_inc(e_used, 1)

            def body(e, last):
                pe.wait_ge(xe_lo_done, 2 * e + 2)
                gate_up(0, e)
                gate_up(1, e)
                hid_transpose(0, e)
                gate_up(2, e)
                hid_transpose(1, e)
                gate_up(3, e)
                hid_transpose(2, e)
                if not last:
                    next_tokens(0, e)
                pe.wait_ge(hT2_lo_done, 4 * e + 1)
                e_wait_free(("d", 0), e)
                e_wait_free(("d", 1), e)
                down(16, e)
                down(17, e)
                hid_transpose(3, e)
                if not last:
                    next_tokens(1, e)
                for u in range(18, EU):
                    if u % 2 == 0:
                        pe.wait_ge(hT2_lo_done, 4 * e + (u - 16) // 2 + 1)
                    down(u, e)

            with pe.Fori(0, NE - 1) as e:
                body(e, False)
            body(NE - 1, True)


_INS = ["x", "in_ln_g", "in_ln_b", "w_in", "b_in", "pool_w", "pool_scale", "sgu_ln_g", "sgu_ln_b", "sgu_w", "sgu_b",
        "p_a", "p_b", "w_out", "ln1_g", "ln1_b", "w_router", "w_gate", "w_up", "w_down", "ln2_g", "ln2_b"]


def kernel(**inputs):
    import numpy as _np
    import concourse.bacc as _bacc
    from concourse import mybir as _mybir
    from concourse.bass_utils import run_bass_kernel_spmd as _run

    nc = _bacc.Bacc("TRN2", target_bir_lowering=False, num_devices=1)
    arrays, args = {}, []
    for name in _INS:
        a = _np.ascontiguousarray(inputs[name])
        arrays[f"in_{name}_dram"] = a
        args.append(nc.dram_tensor(f"in_{name}_dram", a.shape, _mybir.dt.from_np(a.dtype), kind="ExternalInput").ap())
    args.append(nc.dram_tensor("out_0_dram", (1, S, D), _mybir.dt.float32, kind="ExternalOutput").ap())
    hybrid_moe_kernel(nc, *args)
    r = _run(nc, [arrays], core_ids=[0])
    return r.results[0]["out_0_dram"]
```

```python
import concourse.bass as bass
from concourse import mybir
from contextlib import ExitStack

FP = mybir.dt.float32
FR = mybir.dt.float32r
U32 = mybir.dt.uint32
U8 = mybir.dt.uint8
ACT = mybir.ActivationFunctionType
ALU = mybir.AluOpType
AX = mybir.AxisListType

P = 128
D = 1024
S = 1024
KT = D // P
MT = S // P
HALF = 512
WINDOWS = (2, 4, 8, 16)
NG = len(WINDOWS)
PW = NG * P
NE = 16
CAP = 2 * S // NE
F = 2 * D
ALPHA = 2.0 ** 0.25
EPS = 1e-5
PAD = 8
PADW = S + 2 * PAD
BLO = 32
ROW = D + NE

C_A, C_U, C_V, C_GA, C_GB = 0, PW, PW + D, PW + 2 * D, PW + 3 * D
N_BIN = (PW + 4 * D) // P
COL_SCALE, COL_G, COL_B = N_BIN, N_BIN + NG, N_BIN + NG + KT
N_COLS = N_BIN + NG + 2 * KT

U_A, U_GA = 0, 4
U_PA = U_GA + 8
U_V = U_PA + 4
U_U = U_V + 16
U_GP = U_U + 8
U_WO = U_GP + 16
U_END = U_WO + KT
GB_PB = [(kind, n) for n in range(KT - 2) for kind in ("gb", "pb")] + [("gb", 6), ("gb", 7), ("pb", 6), ("pb", 7)]
EU = 24
NRAW = 12
NSPLIT = 3


def hybrid_moe_kernel(nc, x, in_ln_g, in_ln_b, w_in, b_in, pool_w, pool_scale, sgu_ln_g, sgu_ln_b,
                      sgu_w, sgu_b, p_a, p_b, w_out, ln1_g, ln1_b, w_router, w_gate, w_up, w_down,
                      ln2_g, ln2_b, out):
    ctx = ExitStack()
    with ctx:
        base = -(-nc.sbuf_base // 32) * 32
        arena = ctx.enter_context(nc.sbuf_tensor("arena", [P, (nc.sbuf_usable_end - base - 32) // 4], FP))
        R_AM = base
        R_HT = R_AM + 32768
        R_VH = R_HT + 65536
        R_VL = R_VH + 32768
        R_WR = R_VL + 32768
        R_WS = R_WR + 8192
        R_T = R_WS + 16384
        R_EX = R_T + 2 * PADW * 4
        R_SM = R_EX + 12288
        top = [R_SM]

        def at(name, shape, off, dt=FP):
            return nc.alloc_sbuf_tensor_at(name, shape, dt, offset=off)

        def small(name, shape, dt=FP):
            n = 4
            for s in shape[1:]:
                n *= s
            off = top[0]
            top[0] += -(-n // 32) * 32
            assert top[0] <= nc.sbuf_usable_end, top[0]
            return at(name, shape, off, dt)

        def sem(name):
            return ctx.enter_context(nc.semaphore(name))

        am = at("am", [P, KT, S], R_AM)
        hT_hi = at("hT_hi", [P, KT, S], R_HT, FR)
        hT_lo = at("hT_lo", [P, KT, S], R_HT + 32768, FR)
        mT = at("mT", [P, MT, 2, KT, P], R_HT, FR)
        v_hi = at("v_hi", [P, KT, MT, P], R_VH, FR)
        v_lo = at("v_lo", [P, KT, MT, P], R_VL, FR)
        v_f = at("v_f", [P, KT, MT, P], R_VL)
        yb_hi = at("yb_hi", [P, KT, S], R_VH, FR)
        yb_lo = at("yb_lo", [P, KT, S], R_VL, FR)
        yb_f = at("yb_f", [P, KT, S], R_VL)
        xr = at("xr", [P, MT, D], R_VL)
        ya_hi = at("ya_hi", [P, NG, S], R_VL, FR)
        ya_lo = at("ya_lo", [P, NG, S], R_VL + 16384, FR)
        h1 = at("h1", [P, MT, D], R_VL)
        R_PA = R_VH + NG * PADW * 4
        g0 = at("g0", [P, D], R_PA)
        b0 = at("b0", [P, D], R_PA + 4096)
        vec_rows = at("vec_rows", [N_COLS, P], R_PA + 10240)
        ws_raw = at("ws_raw", [P, KT, P], R_VH)
        sb_row = at("sb_row", [P, KT, P], R_VH + 4096)
        wsT = at("wsT", [P, KT, P], R_VH + 8192)
        bv_raw = at("bv_raw", [BLO + 1, D], R_VH + 12288)
        apad = at("apad", [P, NG, PADW], R_VH)
        pa_hi = at("pa_hi", [P, S], R_PA, FR)
        pa_lo = at("pa_lo", [P, S], R_PA + 4096, FR)
        pw_raw = at("pw_raw", [P, NG, P], R_PA + 8192)
        pw_hi = at("pw_hi", [P, NG, P], R_PA + 10240, FR)
        pw_lo = at("pw_lo", [P, NG, P], R_PA + 12288, FR)
        g1 = at("g1", [P, D], R_VH + 24576)
        b1 = at("b1", [P, D], R_VH + 28672)
        h1T = at("h1T", [P, 2, KT, P], R_T)
        ah = at("ah", [P, 2, D], R_WR)
        wr = at("wr", [P, 2, 1024], R_WR)
        wh = at("wh", [P, 2, 1024], R_WS, FR)
        wl = at("wl", [P, 2, 1024], R_WS + 8192, FR)
        wa_hi = at("wa_hi", [P, NG, 1024], R_AM, FR)
        wa_lo = at("wa_lo", [P, NG, 1024], R_AM + 16384, FR)
        wo_off = [R_AM, R_AM + 8192, R_AM + 16384, None, None, R_VH, R_VH + 8192, R_VH + 16384]
        wo_hi = [at(f"wo_hi{k}", [P, 1024], o, FR) if o is not None else wh[:, k - 3, :] for k, o in enumerate(wo_off)]
        wo_lo = [at(f"wo_lo{k}", [P, 1024], o + 4096, FR) if o is not None else wl[:, k - 3, :] for k, o in enumerate(wo_off)]
        tt = [at(f"tt{i}", [P, PADW], R_T + i * PADW * 4) for i in range(2)]
        bv = at("bv", [BLO + 1, D], R_T + PADW * 4, FR)
        rr = at("rr", [P, KT, P], R_EX)
        ws_hi = at("ws_hi", [P, KT, P], R_EX + 4096, FR)
        ws_lo = at("ws_lo", [P, KT, P], R_EX + 8192, FR)
        affT = at("affT", [NE, S], R_EX)
        cs = at("cs", [NE, S], R_EX + 4096, U8)
        sel = at("sel", [NE, S], R_EX + 8192)
        g2 = at("g2", [P, D], R_EX)
        b2 = at("b2", [P, D], R_EX + 4096)
        aff = at("aff", [P, MT, NE], R_EX + 8192)
        raw = at("raw", [P, NRAW, 2048], R_AM)
        eh = [at(f"eh{i}", [P, 2048], R_VH + 16384 * i, FR) for i in range(NSPLIT)]
        el = [at(f"el{i}", [P, 2048], R_VH + 16384 * i + 8192, FR) for i in range(NSPLIT)]
        hidT_hi = at("hidT_hi", [P, F // P, P], R_VL + 16384, FR)
        hidT_lo = at("hidT_lo", [P, F // P, P], R_VL + 24576, FR)
        xeT_hi = at("xeT_hi", [P, KT, P], R_WR, FR)
        xeT_lo = at("xeT_lo", [P, KT, P], R_WR + 4096, FR)
        xe = at("xe", [P, ROW], R_WR + 8192)
        cs_r = at("cs_r", [NE, S], R_WR + 8192 + 4160, FR)
        hid = at("hid", [P, 2, HALF], R_WR + 8192 + 4160)
        sil = at("sil", [P, 2, HALF], R_WR + 8192 + 4160 + 4096)
        ye = at("ye", [P, D], R_T)
        csb = at("csb", [P, S], R_T + 4096, U8)
        fin = at("fin", [P, MT, D], R_HT)

        ident = small("ident", [P, P])
        cols = small("cols", [P, N_COLS])
        edge = small("edge", [P, NG, 2 * PAD])
        ones = small("ones", [P, P])
        ones_r = small("ones_r", [BLO + 1, P], FR)
        w_rt = small("w_rt", [P, KT, NE])
        idx_h = small("idx_h", [P, 2])
        stat = small("stat", [P, 2, 2, 6])
        mean = small("mean", [P, 2, 2])
        veps = small("veps", [P, 2])
        rstd = small("rstd", [P, 2])
        mhalf = small("mhalf", [P, 1])
        nmax = small("nmax", [P, 1])
        esum = small("esum", [P, 1])
        rsum = small("rsum", [P, 1])
        top8 = small("top8", [NE, 8])
        slot_no = small("slot_no", [P, 1])
        idx_f = small("idx_f", [P, 1])
        idx_g = small("idx_g", [P, 1], U32)
        idx_m = small("idx_m", [P, 1], U32)
        idx_s = small("idx_s", [P, 1], U32)
        gate_g = small("gate_g", [P, 1])
        gate_s = small("gate_s", [P, 1])
        ps = [ctx.enter_context(nc.psum_tensor(f"ps{i}", [P, HALF], FP)) for i in range(8)]

        h0_dram = nc.dram_tensor("h0_rows", (S, D), FP, kind="Internal").ap()
        hx_dram = nc.dram_tensor("h1_rows", (S, ROW), FP, kind="Internal").ap()
        acc_dram = nc.dram_tensor("acc_rows", (S, D), FP, kind="Internal").ap()
        cs_dram = nc.dram_tensor("cs_rows", (NE, S), U8, kind="Internal").ap()

        psum_full = [sem(f"psum_full{i}") for i in range(8)]
        psum_free = [sem(f"psum_free{i}") for i in range(8)]
        cs_r_done = sem("cs_r_done")
        affine_dve, rs_done = sem("affine_dve"), sem("rs_done")
        bvr_ok, bv_hi_done, bv_done, ones_r_done = (sem(n) for n in ("bv_zeroed", "bv_hi_done", "bv_done", "ones_r_done"))
        x_in = [sem(f"x_in{i}") for i in range(MT)]
        vec_in, ws_in, sb_in, g0_in, b0_in, pw_in, bv_in, ln1_in, ln2_in, rt_in = (
            sem(n) for n in ("vec_in", "ws_in", "sb_in", "g0_in", "b0_in", "pw_in", "bv_in", "ln1_in", "ln2_in", "rt_in"))
        h0_in = [sem(f"h0_in{i}") for i in range(MT)]
        fin_in = [sem(f"fin_in{i}") for i in range(MT)]
        w_in_s = [sem(f"w_landed{i}") for i in range(2)]
        w_hi_done, w_lo_done, w_used = sem("w_hi_done"), sem("w_lo_done"), sem("w_used")
        consts, ident_ok = sem("consts"), sem("ident_ok")
        stats_done, rstd_done, norm_done, affine_done = (
            sem(n) for n in ("stats_done", "rstd_done", "norm_done", "affine_done"))
        cols_done, wsT_done, ws_lo_done, rr_done = (sem(n) for n in ("cols_done", "wsT_done", "ws_lo_done", "rr_done"))
        ws_hi_done = sem("ws_hi_done")
        hT_hi_done, hT_lo_done = sem("hT_hi_done"), sem("hT_lo_done")
        pad_done, apad_done = sem("pad_done"), sem("apad_done")
        pw_hi_done, pw_lo_done, pa_f_done, pa_hi_done, pa_lo_done = (
            sem(n) for n in ("pw_hi_done", "pw_lo_done", "pa_f_done", "pa_hi_done", "pa_lo_done"))
        ya_hi_done, ya_lo_done, am_done = (sem(n) for n in ("ya_hi_done", "ya_lo_done", "am_done"))
        v_gelu_done, v_hi_done, v_lo_done = (sem(n) for n in ("v_gelu_done", "v_hi_done", "v_lo_done"))
        gu_done, yb_f_done, yb_hi_done, yb_lo_done = (
            sem(n) for n in ("gu_done", "yb_f_done", "yb_hi_done", "yb_lo_done"))
        sgb_done, mg_hi_done, mg_lo_done = sem("sgb_done"), sem("mg_hi_done"), sem("mg_lo_done")
        h0_stored, h1_stored, aff_stored, cs_stored, out_stored = (
            sem(n) for n in ("h0_stored", "h1_stored", "aff_stored", "cs_stored", "out_stored"))
        acc_stored = [sem(f"acc_stored{i}") for i in range(2)]
        ah_done, h1T_done, nmax_done, exp_done, aff_done, affT_done, cs_done = (
            sem(n) for n in ("ah_done", "h1T_done", "nmax_done", "exp_done", "aff_done", "affT_done", "cs_done"))
        raw_in = [sem(f"raw_in{i}") for i in range(NRAW)]
        e_hi_done, e_lo_done, e_used = sem("e_hi_done"), sem("e_lo_done"), sem("e_used")
        e_lo_first = sem("e_lo_first")
        gate_s_done, idx_m_done = sem("gate_s_done"), sem("idx_m_done")
        csb_in, idx_done, idx_s_done, gathered, gate_done, scattered = (
            sem(n) for n in ("csb_in", "idx_done", "idx_s_done", "gathered", "gate_done", "scattered"))
        xe_hi_done, xe_lo_done, sil_done, hid_done, hT2_hi_done, hT2_lo_done, ye_done = (
            sem(n) for n in ("xe_hi_done", "xe_lo_done", "sil_done", "hid_done", "hidT_hi_done", "hidT_lo_done", "ye_done"))
        waits_held = {nc.sync.engine: sem("sp_held"), nc.gpsimd.engine: sem("pool_held")}
        dve_step, pool_step = sem("dve_step"), sem("pool_step")

        order = ["cols"] + [("h", m, i) for m in range(4) for i in range(2)]
        for g in range(NG):
            order += [("a", g, 0), ("h", 4 + g, 0), ("h", 4 + g, 1)]
        order += [("a", g, 1) for g in range(NG)]
        for n in range(KT):
            order += [("ga", n, i) for i in range(2)]
            if 2 <= n < 2 + NG:
                order += [("ya", n - 2, i) for i in range(2)]
        order += [("ws", 0), ("ws", 1)]
        for n in range(KT):
            order += [("pa", n, i) for i in range(2)]
            if n == 1:
                order += [("rw", 0), ("rw", 1)]
        for grp in range(2):
            order += [("v", m, j) for m in range(4 * grp, 4 * grp + 4) for j in range(2)]
        order += [("u", 0, 0), ("u", 0, 1)]
        for h in range(KT):
            if h + 1 < KT:
                order += [("u", h + 1, 0), ("u", h + 1, 1)]
            order += [("mix", h, 0), ("mix", h, 1)]
        for kind, n in GB_PB:
            order += [(kind, n, 0), (kind, n, 1)]
        order += [("wo", m, j) for m in range(2) for j in range(2)]
        t, lg, a_t = (lambda m: ("t", m)), (lambda m: ("lg", m)), (lambda m: ("at", m))
        route_steps = [("wo", 2, 0), ("wo", 2, 1), t(0), ("wo", 3, 0), lg(0), t(1), ("wo", 3, 1), a_t(0), lg(1)]
        for m in range(4, MT):
            route_steps += [("wo", m, 0), t(m - 2), a_t(m - 3), ("wo", m, 1)] + ([lg(m - 2)] if m < MT - 1 else [])
        route_steps += [t(6), lg(5), lg(6), a_t(5), t(7), a_t(6), lg(7), a_t(7)]
        for step in route_steps:
            order += [("t", step[1], 0), ("t", step[1], 1)] if step[0] == "t" else [step]
        order += [("cb", 0), ("cb", 1), ("xt", 0), ("xt", 1)]
        JOB = {name: q for q, name in enumerate(order)}
        Q0 = len(order)
        e_order = [("g", 0), ("u", 0), ("g", 1), ("u", 1), ("t", 0), ("g", 2), ("u", 2), ("t", 1), ("g", 3), ("u", 3),
                   ("t", 2), ("x", 0), ("d", 0), ("d", 1), ("t", 3), ("x", 1)]
        EJOB = {name: Q0 + c for c, name in enumerate(e_order)}

        def bank(name):
            return ps[JOB[name] % 8]

        def wait_full(eng, name):
            q = JOB[name]
            eng.wait_ge(psum_full[q % 8], q // 8 + 1)

        def wait_free(name):
            q = JOB[name]
            if q >= 8:
                nc.tensor.wait_ge(psum_free[q % 8], q // 8)

        def full(name):
            return psum_full[JOB[name] % 8]

        def free(name):
            return psum_free[JOB[name] % 8]

        def ebank(name):
            return ps[EJOB[name] % 8]

        def e_wait_full(eng, name, e):
            q = EJOB[name]
            eng.wait_ge(psum_full[q % 8], q // 8 + 1 + 2 * e)

        def e_wait_free(name, e):
            q = EJOB[name]
            nc.tensor.wait_ge(psum_free[q % 8], q // 8 + 2 * e)

        def e_full(name):
            return psum_full[EJOB[name] % 8]

        def e_free(name):
            return psum_free[EJOB[name] % 8]

        last_job, used_no = {}, {}
        for n in range(KT):
            last_job[U_GA + n] = ("ga", n, 1)
            last_job[U_U + n] = ("u", n, 1)
        for i, (kind, n) in enumerate(GB_PB):
            last_job[U_GP + i] = (kind, n, 1)
        for n in range(4):
            last_job[U_PA + n] = ("pa", 2 * n + 1, 1)
        for grp in range(2):
            last_job[U_V + 8 * grp + 7] = ("v", 4 * grp + 3, 1)
        for i in range(U_V, U_U):
            if i not in last_job:
                used_no[i] = len(used_no) + 1

        def wait_unit_used(eng, i):
            if i in last_job:
                wait_full(eng, last_job[i])
            else:
                eng.wait_ge(w_used, used_no[i])

        def halves(i):
            if i < U_GA:
                return wa_hi[:, i, :], wa_lo[:, i, :]
            if i >= U_WO:
                return wo_hi[i - U_WO][:], wo_lo[i - U_WO][:]
            return wh[:, i % 2, :], wl[:, i % 2, :]

        def wait_halves_free(eng, i):
            k = i - U_WO
            if k >= 5:
                wait_full(eng, ("pb", KT - 1, 1))
            elif k >= 3:
                wait_unit_used(eng, U_WO - 5 + k)
            elif k >= 0:
                eng.wait_ge(mg_lo_done, 2 * k + 2)
            elif i >= U_GA + 2:
                wait_unit_used(eng, i - 2)

        def raw_slot(u):
            return (u + 3) % NRAW

        def e_wait_used(eng, u, e):
            if u < 16 and u % 2:
                e_wait_full(eng, ("gu"[u // 2 % 2], u // 4), e)
            elif u == EU - 1:
                e_wait_full(eng, ("d", 1), e)
            else:
                eng.wait_ge(e_used, 15 * e + (u // 2 + 1 if u < 16 else u - 7))

        w_in_v = w_in[0].rearrange("(k p) n -> p k n", p=P)
        pa_v = p_a[0].rearrange("(k p) n -> p k n", p=P)
        pb_v = p_b[0].rearrange("(k p) n -> p k n", p=P)

        def unit_source(i):
            if i < U_GA:
                return w_in_v[:, :, C_A + P * i:C_A + P * i + P]
            if i < U_PA:
                return w_in_v[:, :, C_GA + P * (i - U_GA):C_GA + P * (i - U_GA) + P]
            if i < U_V:
                return pa_v[:, :, 2 * P * (i - U_PA):2 * P * (i - U_PA) + 2 * P]
            if i < U_U:
                return w_in_v[:, (i - U_V) % 8, C_V:C_V + D]
            if i < U_GP:
                return w_in_v[:, :, C_U + P * (i - U_U):C_U + P * (i - U_U) + P]
            if i < U_WO:
                kind, n = GB_PB[i - U_GP]
                v = pb_v if kind == "pb" else w_in_v[:, :, C_GB:C_GB + D]
                return v[:, :, P * n:P * n + P]
            k = i - U_WO
            return w_out[0, P * k:P * k + P, :]

        def as_source(t, i):
            if U_PA <= i < U_V:
                return t.rearrange("p (k n) -> p k n", n=2 * P)
            if U_V <= i < U_U or i >= U_WO:
                return t
            return t.rearrange("p (k n) -> p k n", n=P)

        wg_v = w_gate[0].rearrange("e (k p) f -> p e k f", p=P)
        wu_v = w_up[0].rearrange("e (k p) f -> p e k f", p=P)
        wd_v = w_down[0].rearrange("e (k p) n -> p e k n", p=P)

        def expert_source(u, e):
            if u < 16:
                j, half = divmod(u, 4)
                v = wu_v if half >= 2 else wg_v
                k = 4 * (half % 2)
                return v[:, bass.ds(e, 1), k:k + 4, HALF * j:HALF * j + HALF].rearrange("p a k f -> p (a k) f")
            k = 2 * (u - 16)
            return wd_v[:, bass.ds(e, 1), k:k + 2, :].rearrange("p a k f -> p (a k) f")

        def held(eng):
            eng.sem_inc(waits_held[eng.engine], 1)

        def flat(t):
            return t.rearrange("p a b -> p (a b)")

        block = ctx.enter_context(nc.Block())

        @block.sync
        def _(sp):
            sp.dma_start(xr[:, 0, :], x[0, 0:P, :]).then_inc(x_in[0], 16)
            sp.dma_start(g0[:], in_ln_g.partition_broadcast(P)).then_inc(g0_in, 16)
            def load_unit(i):
                if i >= 2:
                    sp.wait_ge(w_lo_done, i - 1)
                sp.dma_start(as_source(wr[:, i % 2, :], i), unit_source(i)).then_inc(w_in_s[i % 2], 16)

            for m in range(1, MT):
                sp.dma_start(xr[:, m, :], x[0, P * m:P * m + P, :]).then_inc(x_in[m], 16)
                if m == 1:
                    sp.dma_start(b0[:], in_ln_b.partition_broadcast(P)).then_inc(b0_in, 16)
                    load_unit(0)
                if m == 3:
                    load_unit(1)
            for i in range(2, U_END):
                load_unit(i)
                if i == 5:
                    for m in range(MT):
                        sp.wait_ge(affine_done, m + 1)
                        sp.dma_start(h0_dram[P * m:P * m + P, :], xr[:, m, :]).then_inc(h0_stored, 16)
            sp.wait_ge(mg_lo_done, KT)
            for u in range(NRAW + NSPLIT):
                if 1 <= u <= MT:
                    wait_full(sp, ("wo", max(u - 1, 1), 1))
                if u >= NRAW:
                    sp.wait_ge(e_lo_first, u - NRAW + 1)
                k = 4 if u < 16 else 2
                sp.dma_start(raw[:, raw_slot(u), :].rearrange("p (k f) -> p k f", k=k), expert_source(u, 0)).then_inc(raw_in[u % NRAW], 16)

            def load(u, e, g):
                sp.wait_ge(e_lo_done, g - NRAW + 1)
                held(sp)
                k = 4 if u < 16 else 2
                sp.dma_start(raw[:, raw_slot(u), :].rearrange("p (k f) -> p k f", k=k), expert_source(u, e)).then_inc(raw_in[u % NRAW], 16)

            with sp.Fori(0, NE - 1) as e:
                for u in range(NRAW + NSPLIT, EU):
                    load(u, e, EU * e + u)
                for u in range(NRAW + NSPLIT):
                    load(u, e + 1, EU * e + EU + u)
            for u in range(NRAW + NSPLIT, EU):
                load(u, NE - 1, EU * (NE - 1) + u)

            sp.wait_ge(scattered, 16 * NE)
            for m in range(MT):
                sp.dma_start(fin[:, m, :], acc_dram[P * m:P * m + P, :]).then_inc(fin_in[m], 16)
            for m in range(MT):
                if m < MT - 1:
                    sp.wait_ge(affine_done, MT + m + 1)
                else:
                    sp.wait_ge(affine_dve, MT + 1)
                sp.dma_start(out[0, P * m:P * m + P, :], fin[:, m, :]).then_inc(out_stored, 16)
            sp.wait_ge(out_stored, 16 * MT)

        @block.gpsimd
        def _(pool):
            steps = [0]

            def link(ins):
                steps[0] += 1
                ins.then_inc(pool_step, 1)
                pool.wait_ge(pool_step, steps[0])

            link(nc.gpsimd.memset(ident[:], 0.0))
            nc.gpsimd.affine_select(out=ident[:], in_=ident[:], compare_op=ALU.not_equal, fill=1.0, base=0,
                                    pattern=[[-1, P]], channel_multiplier=1).then_inc(ident_ok, 1)
            nc.gpsimd.memset(mhalf[:], -0.5).then_inc(consts, 1)
            nc.gpsimd.memset(ones[:], 1.0).then_inc(consts, 1)
            nc.gpsimd.iota(slot_no[:], [[0, 1]], base=0, channel_multiplier=1,
                           allow_small_or_imprecise_dtypes=True).then_inc(consts, 1)
            nc.gpsimd.memset(apad[:, :, 0:PAD], 0.0).then_inc(pad_done, 1)
            nc.gpsimd.memset(apad[:, :, PAD + S:PADW], 0.0).then_inc(pad_done, 1)

            def rsqrt(i):
                pool.wait_ge(stats_done, i + 1)
                nc.gpsimd.tensor_tensor(rstd[:, i % 2:i % 2 + 1], veps[:, i % 2:i % 2 + 1], mhalf[:], ALU.pow).then_inc(rstd_done, 1)

            def bias_add(t, b, n):
                pool.wait_ge(rs_done, n + 1)
                nc.gpsimd.tensor_tensor(t, t, b, ALU.add).then_inc(affine_done, 1)

            pool.wait_ge(consts, 3)
            rsqrt(0)
            pool.wait_ge(b0_in, 16)
            for m in range(MT):
                if m + 1 < MT:
                    rsqrt(m + 1)
                bias_add(xr[:, m, :], b0[:], m)
            wait_full(pool, "cols")
            pool.dma_start(pw_raw[:], pool_w[0].rearrange("g c d -> c g d")).then_inc(pw_in, 16)
            nc.gpsimd.memset(edge[:], 1.0).then_inc(consts, 1)
            pool.wait_ge(consts, 4)
            for g, w in enumerate(WINDOWS):
                for t in range(w // 2):
                    nc.gpsimd.memset(edge[:, g, t:t + 1], w / (t + w // 2)).then_inc(consts, 1)
                for t in range(S - w // 2 + 1, S):
                    nc.gpsimd.memset(edge[:, g, t - S + 2 * PAD:t - S + 2 * PAD + 1], w / (S - t + w // 2)).then_inc(consts, 1)
            pool.wait_ge(pa_f_done, NG)
            pool.dma_start(ws_raw[:], sgu_w[0].rearrange("h p q -> p h q")).then_inc(ws_in, 16)
            pool.dma_start(sb_row[:].rearrange("p h q -> p (h q)"),
                           sgu_b[0].rearrange("h p -> (h p)").partition_broadcast(P)).then_inc(sb_in, 16)
            nc.gpsimd.memset(bv_raw[:], 0.0).then_inc(bvr_ok, 1)
            pool.wait_ge(bvr_ok, 1)
            for r in (0, BLO):
                pool.dma_start(bv_raw[r:r + 1, :], b_in[0:1, C_V:C_V + D]).then_inc(bv_in, 16)
            for m in range(MT):
                rsqrt(MT + m)
            wait_full(pool, ("pb", KT - 1, 1))
            pool.wait_ge(h0_stored, 16 * MT)
            pool.dma_start(g1[:], ln1_g[0].partition_broadcast(P)).then_inc(ln1_in, 16)
            pool.dma_start(b1[:], ln1_b[0].partition_broadcast(P)).then_inc(ln1_in, 16)
            pool.dma_start(w_rt[:], w_router[0].rearrange("(k p) e -> p k e", p=P)).then_inc(rt_in, 16)
            for m in range(MT):
                pool.dma_start(h1[:, m, :], h0_dram[P * m:P * m + P, :]).then_inc(h0_in[m], 16)
            pool.wait_ge(ln1_in, 32)
            for m in range(MT):
                rsqrt(2 * MT + m)

            def lo_part(u):
                pool.wait_ge(e_hi_done, u + 1)
                nc.gpsimd.tensor_tensor(el[u][:], raw[:, raw_slot(u), :], eh[u][:].bitcast(FP), ALU.subtract).then_inc(e_lo_first, 1)

            for u in range(NSPLIT):
                lo_part(u)
            pool.wait_ge(cs_done, 1)
            pool.dma_start(cs_dram[:, :], cs[:]).then_inc(cs_stored, 16)
            pool.wait_ge(h1_stored, 16 * MT)
            pool.wait_ge(aff_stored, 16)

            def load_counts(e):
                pool.dma_start(csb[:], cs_dram[bass.ds(e, 1), :].rearrange("a s -> (a s)").partition_broadcast(P)).then_inc(csb_in, 16)

            def gather(e):
                pool.wait_ge(idx_done, e + 1)
                held(pool)
                nc.gpsimd.indirect_dma_start(out=xe[:], out_offset=None, in_=hx_dram[:, :],
                                             in_offset=bass.IndirectOffsetOnAxis(ap=idx_g[:], axis=0)).then_inc(gathered, 16)

            def keep_gates(e):
                pool.wait_ge(gathered, 16 * e + 16)
                pool.wait_ge(gate_s_done, e)
                held(pool)
                nc.gpsimd.tensor_copy(gate_g[:], xe[:, bass.ds(D + e, 1)]).then_inc(gate_done, 1)

            gather(0)
            pool.wait_ge(cs_stored, 16)
            load_counts(1)
            for i in range(2):
                pool.wait_ge(acc_stored[i], 16 * MT // 2)
            pool.dma_start(g2[:], ln2_g[0].partition_broadcast(P)).then_inc(ln2_in, 16)
            pool.dma_start(b2[:], ln2_b[0].partition_broadcast(P)).then_inc(ln2_in, 16)
            pool.wait_ge(gathered, 16)
            nc.gpsimd.tensor_copy(gate_g[:], xe[:, D:D + 1]).then_inc(gate_done, 1)

            def body(e, left, first=False):
                pool.wait_ge(gate_done, e + 1)
                if not first:
                    pool.wait_ge(idx_s_done, e)
                    held(pool)
                nc.gpsimd.tensor_copy(idx_m[:], idx_g[:]).then_inc(idx_m_done, 1)
                if left > 0:
                    gather(e + 1)
                if left > 1:
                    load_counts(e + 2)
                if not first:
                    pool.wait_ge(scattered, 16 * e)
                    pool.wait_ge(ye_done, 2 * e)
                pool.wait_ge(idx_m_done, e + 1)
                held(pool)
                nc.gpsimd.tensor_copy(gate_s[:], gate_g[:]).then_inc(gate_s_done, 1)
                nc.gpsimd.tensor_copy(idx_s[:], idx_m[:]).then_inc(idx_s_done, 1)
                if left > 0:
                    keep_gates(e + 1)
                pool.wait_ge(ye_done, 2 * e + 2)
                pool.wait_ge(idx_s_done, e + 1)
                held(pool)
                nc.gpsimd.indirect_dma_start(out=acc_dram[:, :], out_offset=bass.IndirectOffsetOnAxis(ap=idx_s[:], axis=0),
                                             in_=ye[:], in_offset=None, compute_op=ALU.add).then_inc(scattered, 16)

            body(0, NE - 1, first=True)
            with pool.Fori(1, NE - 2) as e:
                body(e, 2)
            body(NE - 2, 1)
            body(NE - 1, 0)

            pool.wait_ge(ln2_in, 32)
            rsqrt(3 * MT)
            for m in range(MT):
                if m + 1 < MT:
                    rsqrt(3 * MT + m + 1)
                if m < MT - 1:
                    bias_add(fin[:, m, :], b2[:], MT + m)

        @block.scalar
        def _(act):
            def w_hi(i):
                act.wait_ge(w_in_s[i % 2], 16 * (i // 2 + 1))
                wait_halves_free(act, i)
                nc.scalar.activation(halves(i)[0], wr[:, i % 2, :], ACT.Copy).then_inc(w_hi_done, 1)

            def rstd_part(t, i, n):
                act.wait_ge(norm_done, n + 1)
                act.wait_ge(rstd_done, i + 1)
                nc.scalar.activation(t, t, ACT.Copy, scale=rstd[:, i % 2:i % 2 + 1]).then_inc(rs_done, 1)

            act.dma_start(vec_rows[0:N_BIN, :], b_in[0].rearrange("(c p) -> c p", p=P)).then_inc(vec_in, 16)
            act.dma_start(vec_rows[COL_SCALE:COL_SCALE + NG, :], pool_scale[0].rearrange("(c p) -> c p", p=P)).then_inc(vec_in, 16)
            act.dma_start(vec_rows[COL_G:COL_G + KT, :], sgu_ln_g[0].rearrange("(c p) -> c p", p=P)).then_inc(vec_in, 16)
            act.dma_start(vec_rows[COL_B:COL_B + KT, :], sgu_ln_b[0].rearrange("(c p) -> c p", p=P)).then_inc(vec_in, 16)
            wait_full(act, "cols")
            nc.scalar.activation(cols[:], bank("cols")[:, 0:N_COLS], ACT.Copy).then_inc(cols_done, 1)
            act.wait_ge(cols_done, 1)
            act.sem_inc(free("cols"), 1)

            def h_hi_part(m):
                for i in range(2):
                    wait_full(act, ("h", m, i))
                    nc.scalar.activation(hT_hi[:, 4 * i:4 * i + 4, P * m:P * m + P],
                                         bank(("h", m, i))[:].rearrange("p (k t) -> p k t", t=P), ACT.Copy).then_inc(hT_hi_done, 1)

            def a_evac(g, i):
                wait_full(act, ("a", g, i))
                act.wait_ge(pad_done, 2)
                nc.scalar.activation(apad[:, g, PAD + HALF * i:PAD + HALF * i + HALF], bank(("a", g, i))[:], ACT.Identity,
                                     bias=cols[:, g:g + 1]).then_inc(apad_done, 1)
                act.wait_ge(apad_done, NG * i + g + 1)
                act.sem_inc(free(("a", g, i)), 1)

            x_rstd = lambda m: rstd_part(xr[:, m, :], m, m)
            x_rstd(0)
            w_hi(0)
            x_rstd(1)
            for m in range(3):
                h_hi_part(m)
                x_rstd(m + 2)
            h_hi_part(3)
            w_hi(1)
            x_rstd(5)
            x_rstd(6)
            h_hi_part(4)
            w_hi(2)
            x_rstd(7)
            for g in range(3):
                a_evac(g, 0)
                h_hi_part(5 + g)
                w_hi(3 + g)
            a_evac(3, 0)
            for g in range(NG):
                a_evac(g, 1)

            def sigmoid_ga(n):
                c = C_GA // P + n
                for i in range(2):
                    wait_full(act, ("ga", n, i))
                    nc.scalar.activation(am[:, n, HALF * i:HALF * i + HALF], bank(("ga", n, i))[:], ACT.Sigmoid,
                                         bias=cols[:, c:c + 1]).then_inc(free(("ga", n, i)), 1)

            def pa_hi_part(g):
                act.wait_ge(pa_f_done, g + 1)
                if g:
                    wait_full(act, ("ya", g - 1, 1))
                nc.scalar.activation(pa_hi[:], tt[0][:, 0:S], ACT.Copy).then_inc(pa_hi_done, 1)

            def ya_hi_part(g):
                for i in range(2):
                    wait_full(act, ("ya", g, i))
                    nc.scalar.activation(ya_hi[:, g, HALF * i:HALF * i + HALF], bank(("ya", g, i))[:], ACT.Copy,
                                         scale=cols[:, COL_SCALE + g:COL_SCALE + g + 1]).then_inc(ya_hi_done, 1)

            act.wait_ge(pw_in, 16)
            nc.scalar.activation(pw_hi[:], pw_raw[:], ACT.Copy).then_inc(pw_hi_done, 1)
            for n in range(KT):
                w_hi(U_GA + n + 2)
                sigmoid_ga(n)
                if 2 <= n < 2 + NG:
                    ya_hi_part(n - 2)
                if 1 <= n < 1 + NG:
                    pa_hi_part(n - 1)
            for i in range(2):
                wait_full(act, ("ws", i))
                nc.scalar.activation(flat(wsT[:, 4 * i:4 * i + 4, :]), bank(("ws", i))[:], ACT.Copy).then_inc(wsT_done, 1)
                nc.scalar.activation(flat(ws_hi[:, 4 * i:4 * i + 4, :]), bank(("ws", i))[:], ACT.Copy).then_inc(ws_hi_done, 1)
            act.wait_ge(consts, 2)
            nc.scalar.activation(ones_r[:], ones[0:BLO + 1, :], ACT.Copy).then_inc(ones_r_done, 1)
            act.wait_ge(bv_in, 32)
            act.wait_ge(pa_lo_done, NG)
            nc.scalar.activation(bv[:], bv_raw[:], ACT.Copy).then_inc(bv_hi_done, 1)
            for i in range(U_PA + 2, U_V + 2):
                w_hi(i)

            def gelu_v(m):
                for j in range(2):
                    wait_full(act, ("v", m, j))
                    nc.scalar.activation(v_f[:, 4 * j:4 * j + 4, m, :], bank(("v", m, j))[:].rearrange("p (h d) -> p h d", d=P),
                                         ACT.Gelu_apprx_tanh).then_inc(v_gelu_done, 1)
                    act.wait_ge(v_gelu_done, 2 * m + j + 1)
                    act.sem_inc(free(("v", m, j)), 1)

            def v_hi_part(m):
                act.wait_ge(norm_done, MT + m + 1)
                if m == 0:
                    act.wait_ge(rr_done, KT)
                    act.wait_ge(bv_done, 1)
                nc.scalar.activation(v_hi[:, :, m, :], v_f[:, :, m, :], ACT.Copy).then_inc(v_hi_done, 1)

            for i in range(U_V + 2, U_V + 9):
                w_hi(i)
            for m in range(3):
                gelu_v(m)
            w_hi(U_V + 9)
            gelu_v(3)
            for m in range(4):
                w_hi(U_V + 10 + m)
                v_hi_part(m)
            for i in range(U_V + 14, U_V + 17):
                w_hi(i)
            for m in range(4, 7):
                gelu_v(m)
            w_hi(U_U + 1)
            gelu_v(7)
            for m in range(4, MT):
                v_hi_part(m)

            def gelu_u(h):
                for i in range(2):
                    wait_full(act, ("u", h, i))
                    if h >= 2:
                        act.wait_ge(yb_f_done, h - 1)
                    nc.scalar.activation(tt[h % 2][:, HALF * i:HALF * i + HALF], bank(("u", h, i))[:], ACT.Gelu_apprx_tanh,
                                         bias=cols[:, C_U // P + h:C_U // P + h + 1]).then_inc(gu_done, 1)
                    act.wait_ge(gu_done, 2 * h + i + 1)
                    act.sem_inc(free(("u", h, i)), 1)

            def yb_hi_part(h):
                act.wait_ge(yb_f_done, h + 1)
                nc.scalar.activation(yb_hi[:, h, :], yb_f[:, h, :], ACT.Copy).then_inc(yb_hi_done, 1)

            gelu_u(0)
            for h in range(KT):
                w_hi(U_U + h + 2)
                if h + 1 < KT:
                    gelu_u(h + 1)
                yb_hi_part(h)

            def sigmoid_gb(n):
                for i in range(2):
                    wait_full(act, ("gb", n, i))
                    if n >= 2:
                        act.wait_ge(am_done, 2 * KT + 2 * n - 2)
                    nc.scalar.activation(tt[n % 2][:, HALF * i:HALF * i + HALF], bank(("gb", n, i))[:], ACT.Sigmoid,
                                         bias=cols[:, C_GB // P + n:C_GB // P + n + 1]).then_inc(sgb_done, 1)
                    act.wait_ge(sgb_done, 2 * n + i + 1)
                    act.sem_inc(free(("gb", n, i)), 1)

            def merged_hi(n):
                act.wait_ge(am_done, 2 * KT + 2 * n + 2)
                nc.scalar.activation(mT[:, :, 0, n, :], am[:, n, :].rearrange("p (m t) -> p m t", t=P), ACT.Copy).then_inc(mg_hi_done, 1)

            for i, (kind, n) in enumerate(GB_PB[:-2]):
                if kind == "gb":
                    sigmoid_gb(n)
                w_hi(U_GP + i + 2)
            for k in range(3):
                merged_hi(2 * k)
                merged_hi(2 * k + 1)
                w_hi(U_WO + k)
            merged_hi(6)
            w_hi(U_WO + 3)
            w_hi(U_WO + 4)
            merged_hi(7)
            for k in range(5, KT):
                w_hi(U_WO + k)

            def row_exp(m):
                act.wait_ge(nmax_done, m + 1)
                nc.scalar.activation(aff[:, m, :], bank(("lg", m))[:, 0:NE], ACT.Exp, bias=nmax[:],
                                     accum_out=esum[:]).then_inc(exp_done, 1)
                act.wait_ge(exp_done, m + 1)
                act.sem_inc(free(("lg", m)), 1)

            def row_out(m):
                act.wait_ge(affine_dve, m + 1)
                if m >= 2:
                    act.wait_ge(acc_stored[m % 2], 16 * (m // 2))
                nc.scalar.activation(ah[:, m % 2, :], h1[:, m, :], ACT.Copy, scale=ALPHA).then_inc(ah_done, 1)
                act.dma_start(hx_dram[P * m:P * m + P, 0:D], h1[:, m, :]).then_inc(h1_stored, 16)
                act.wait_ge(ah_done, m + 1)
                act.dma_start(acc_dram[P * m:P * m + P, :], ah[:, m % 2, :]).then_inc(acc_stored[m % 2], 16)

            def route_1(m):
                for i in range(2):
                    wait_full(act, ("t", m, i))
                    nc.scalar.activation(flat(h1T[:, m % 2, 4 * i:4 * i + 4, :]), bank(("t", m, i))[:], ACT.Copy).then_inc(h1T_done, 1)
                    act.wait_ge(h1T_done, 2 * m + i + 1)
                    act.sem_inc(free(("t", m, i)), 1)

            def route_2(m):
                wait_full(act, ("at", m))
                nc.scalar.activation(affT[:, P * m:P * m + P], bank(("at", m))[0:NE, 0:P], ACT.Copy).then_inc(affT_done, 1)
                act.wait_ge(affT_done, m + 1)
                act.sem_inc(free(("at", m)), 1)

            act.wait_ge(w_lo_done, U_END)
            act.wait_ge(am_done, 4 * KT)
            row_out(0)
            row_out(1)
            route_1(0)
            row_exp(0)
            for m in range(1, 6):
                route_1(m)
                row_out(m + 1)
                route_2(m - 1)
                if m < 5:
                    row_exp(m)
            route_1(6)
            row_exp(5)
            row_exp(6)
            route_2(5)
            route_1(7)
            route_2(6)
            row_exp(7)
            route_2(7)
            act.wait_ge(aff_done, MT)
            act.dma_start(hx_dram[:, D:ROW].rearrange("(m p) e -> p m e", p=P), aff[:]).then_inc(aff_stored, 16)

            def e_hi(u, s, g, e_cur, wait_used=True):
                act.wait_ge(raw_in[u % NRAW], s + 16)
                if wait_used:
                    prev = u - NSPLIT
                    e_wait_used(act, prev % EU, e_cur if prev >= 0 else e_cur - 1)
                nc.scalar.activation(eh[u % NSPLIT][:], raw[:, raw_slot(u), :], ACT.Copy).then_inc(e_hi_done, 1)

            row_out(7)
            e_hi(0, 0, 0, 0, wait_used=False)
            e_hi(1, 0, 1, 0, wait_used=False)
            act.wait_ge(h1_stored, 16 * MT)
            e_hi(2, 0, 2, 0, wait_used=False)

            act.wait_ge(cs_r_done, 1)
            nc.scalar.activation(cs[:], cs_r[:].bitcast(FP), ACT.Copy).then_inc(cs_done, 1)

            def x_hi(src, i, waiter):
                waiter()
                nc.scalar.activation(flat(xeT_hi[:, 4 * i:4 * i + 4, :]), src, ACT.Copy).then_inc(xe_hi_done, 1)

            for i in range(2):
                act.wait_ge(acc_stored[i], 16 * MT // 2)
            for i in range(2):
                x_hi(bank(("xt", i))[:], i, lambda: wait_full(act, ("xt", i)))

            def silu(j, e):
                e_wait_full(act, ("g", j), e)
                nc.scalar.activation(sil[:, j % 2, :], ebank(("g", j))[:], ACT.Silu).then_inc(sil_done, 1)
                act.wait_ge(sil_done, 4 * e + j + 1)
                act.sem_inc(e_free(("g", j)), 1)

            def hidT_hi_part(j, e):
                e_wait_full(act, ("t", j), e)
                nc.scalar.activation(flat(hidT_hi[:, 4 * j:4 * j + 4, :]), ebank(("t", j))[:], ACT.Copy).then_inc(hT2_hi_done, 1)

            def body(e, last):
                for u in range(NSPLIT, EU):
                    e_hi(u, 32 * e + 16 * (u // NRAW), EU * e + u, e)
                    if u in (6, 10, 14):
                        silu((u - 6) // 4, e)
                    if u in (10, 14, 18, 21):
                        hidT_hi_part((10, 14, 18, 21).index(u), e)
                    if u == 18:
                        silu(3, e)
                    if not last and u in (18, 21):
                        i = (18, 21).index(u)
                        x_hi(ebank(("x", i))[:], i, lambda: e_wait_full(act, ("x", i), e))
                if not last:
                    for u in range(NSPLIT):
                        e_hi(u, 32 * (e + 1), EU * e + EU + u, e + 1)
                act.wait_ge(idx_s_done, e + 1)
                act.wait_ge(gate_s_done, e + 1)
                for i in range(2):
                    e_wait_full(act, ("d", i), e)
                    nc.scalar.activation(ye[:, HALF * i:HALF * i + HALF], ebank(("d", i))[:], ACT.Copy,
                                         scale=gate_s[:]).then_inc(ye_done, 1)
                act.wait_ge(ye_done, 2 * e + 2)
                act.sem_inc(e_free(("d", 0)), 1)
                act.sem_inc(e_free(("d", 1)), 1)

            with act.Fori(0, NE - 1) as e:
                body(e, False)
            body(NE - 1, True)

            for m in range(MT - 1):
                rstd_part(fin[:, m, :], 3 * MT + m, 2 * MT + m)

        @block.vector
        def _(dve):
            steps = [0]

            def link(ins):
                steps[0] += 1
                ins.then_inc(dve_step, 1)
                dve.wait_ge(dve_step, steps[0])

            def w_lo(i):
                dve.wait_ge(w_hi_done, i + 1)
                hi, lo = halves(i)
                nc.vector.tensor_tensor(lo, wr[:, i % 2, :], hi.bitcast(FP), ALU.subtract).then_inc(w_lo_done, 1)

            def stats(lo_half, hi_half, i):
                s = i % 2
                if i >= 2:
                    dve.wait_ge(rstd_done, i - 1)
                nc.vector.bn_stats(stat[:, s, 0, :], lo_half)
                link(nc.vector.bn_stats(stat[:, s, 1, :], hi_half))
                link(nc.vector.bn_aggr(mean[:, s, :], stat[:, s, :, :]))
                nc.vector.tensor_scalar(veps[:, s:s + 1], mean[:, s, 1:2], EPS, None, ALU.add).then_inc(stats_done, 1)

            def center(t, i):
                s = i % 2
                dve.wait_ge(rstd_done, i + 1)
                return nc.vector.tensor_scalar(t, t, mean[:, s, 0:1], rstd[:, s:s + 1], ALU.subtract, ALU.mult)

            def scale(t, g, i):
                s = i % 2
                return nc.vector.scalar_tensor_tensor(out=t, in0=t, scalar=mean[:, s, 0:1], in1=g, op0=ALU.subtract, op1=ALU.mult)

            def affine(t, b, i):
                s = i % 2
                dve.wait_ge(rstd_done, i + 1)
                return nc.vector.scalar_tensor_tensor(out=t, in0=t, scalar=rstd[:, s:s + 1], in1=b, op0=ALU.mult, op1=ALU.add)

            def hT_lo_part(m):
                for i in range(2):
                    dve.wait_ge(hT_hi_done, 2 * m + i + 1)
                    nc.vector.tensor_tensor(hT_lo[:, 4 * i:4 * i + 4, P * m:P * m + P],
                                            bank(("h", m, i))[:].rearrange("p (k t) -> p k t", t=P),
                                            hT_hi[:, 4 * i:4 * i + 4, P * m:P * m + P].bitcast(FP),
                                            ALU.subtract).then_inc(hT_lo_done, 1)
                    dve.wait_ge(hT_lo_done, 2 * m + i + 1)
                    dve.sem_inc(free(("h", m, i)), 1)

            def x_norm(m):
                dve.wait_ge(x_in[m], 16)
                stats(xr[:, m, 0:HALF], xr[:, m, HALF:D], m)
                if m == 0:
                    dve.wait_ge(g0_in, 16)
                scale(xr[:, m, :], g0[:], m).then_inc(norm_done, 1)

            x_norm(0)
            x_norm(1)
            w_lo(0)
            x_norm(2)
            hT_lo_part(0)
            x_norm(3)
            hT_lo_part(1)
            x_norm(4)
            hT_lo_part(2)
            hT_lo_part(3)
            w_lo(1)
            x_norm(5)
            x_norm(6)
            hT_lo_part(4)
            w_lo(2)
            x_norm(7)
            for m in range(5, MT):
                hT_lo_part(m)
                w_lo(m - 2)

            def pool_group(g):
                w = WINDOWS[g]
                dve.wait_ge(apad_done, NG + g + 1)
                if g:
                    dve.wait_ge(pa_hi_done, g)
                    dve.wait_ge(pa_lo_done, g)
                src, n, width, step = apad[:, g, :], PADW, 1, 0
                side = 0 if (g + 1) % 2 else 1
                while width < w:
                    n -= width
                    dst = tt[side]
                    if 2 * width == w:
                        s0 = PAD - w // 2
                        link(nc.vector.tensor_tensor(dst[:, 0:S], src[:, s0:s0 + S], src[:, s0 + width:s0 + width + S], ALU.add))
                    else:
                        link(nc.vector.tensor_tensor(dst[:, 0:n], src[:, 0:n], src[:, width:width + n], ALU.add))
                    src = dst
                    side ^= 1
                    width *= 2
                assert src is tt[0]
                for a, b, c in ((0, PAD, 0), (S - PAD, S, PAD)):
                    ins = nc.vector.tensor_tensor(tt[0][:, a:b], tt[0][:, a:b], edge[:, g, c:c + PAD], ALU.mult)
                    link(ins)
                nc.vector.scalar_tensor_tensor(out=tt[0][:, 0:S], in0=tt[0][:, 0:S], scalar=1.0 / w,
                                               in1=apad[:, g, PAD:PAD + S], op0=ALU.mult, op1=ALU.subtract).then_inc(pa_f_done, 1)

            def pa_lo_part(g):
                dve.wait_ge(pa_hi_done, g + 1)
                dve.wait_ge(pa_f_done, g + 1)
                nc.vector.tensor_tensor(pa_lo[:], tt[0][:, 0:S], pa_hi[:].bitcast(FP), ALU.subtract).then_inc(pa_lo_done, 1)

            def ya_lo_part(g):
                for i in range(2):
                    dve.wait_ge(ya_hi_done, 2 * g + i + 1)
                    nc.vector.scalar_tensor_tensor(out=ya_lo[:, g, HALF * i:HALF * i + HALF], in0=bank(("ya", g, i))[:],
                                                   scalar=cols[:, COL_SCALE + g:COL_SCALE + g + 1],
                                                   in1=ya_hi[:, g, HALF * i:HALF * i + HALF].bitcast(FP),
                                                   op0=ALU.mult, op1=ALU.subtract).then_inc(ya_lo_done, 1)
                    dve.wait_ge(ya_lo_done, 2 * g + i + 1)
                    dve.sem_inc(free(("ya", g, i)), 1)

            dve.wait_ge(consts, 4 + sum(w - 1 for w in WINDOWS))
            dve.wait_ge(pw_hi_done, 1)
            nc.vector.tensor_tensor(pw_lo[:], pw_raw[:], pw_hi[:].bitcast(FP), ALU.subtract).then_inc(pw_lo_done, 1)
            for n in range(KT):
                w_lo(U_GA + n + 2)
                if 1 <= n < 1 + NG:
                    pa_lo_part(n - 1)
                if n < NG:
                    pool_group(n)
                if 2 <= n < 2 + NG:
                    ya_lo_part(n - 2)

            def pa_merge(n):
                for i in range(2):
                    wait_full(dve, ("pa", n, i))
                    s = slice(HALF * i, HALF * i + HALF)
                    nc.vector.tensor_tensor(am[:, n, s], am[:, n, s], bank(("pa", n, i))[:], ALU.mult).then_inc(am_done, 1)
                    dve.wait_ge(am_done, 2 * n + i + 1)
                    dve.sem_inc(free(("pa", n, i)), 1)

            for i in range(2):
                dve.wait_ge(ws_hi_done, i + 1)
                nc.vector.tensor_tensor(flat(ws_lo[:, 4 * i:4 * i + 4, :]), bank(("ws", i))[:],
                                        flat(ws_hi[:, 4 * i:4 * i + 4, :]).bitcast(FP), ALU.subtract).then_inc(ws_lo_done, 1)
                dve.wait_ge(ws_lo_done, i + 1)
                dve.sem_inc(free(("ws", i)), 1)
            dve.wait_ge(bv_hi_done, 1)
            nc.vector.tensor_tensor(bv[BLO:BLO + 1, :], bv_raw[BLO:BLO + 1, :], bv[BLO:BLO + 1, :].bitcast(FP),
                                    ALU.subtract).then_inc(bv_done, 1)
            for i in range(4):
                w_lo(U_PA + i + 2)
                if i == 1:
                    dve.wait_ge(sb_in, 16)
                    dve.wait_ge(cols_done, 1)
                    for h in range(KT):
                        wait_full(dve, ("rw", h // 4))
                        nc.vector.scalar_tensor_tensor(out=rr[:, h, :], in0=bank(("rw", h // 4))[:, P * (h % 4):P * (h % 4) + P],
                                                       scalar=cols[:, COL_B + h:COL_B + h + 1], in1=sb_row[:, h, :],
                                                       op0=ALU.mult, op1=ALU.add).then_inc(rr_done, 1)
                        if h % 4 == 3:
                            dve.wait_ge(rr_done, h + 1)
                            dve.sem_inc(free(("rw", h // 4)), 1)
                for ct in range(2):
                    pa_merge(2 * i + ct)

            def v_stats(m):
                dve.wait_ge(v_gelu_done, 2 * m + 2)
                stats(v_f[:, 0:4, m, :], v_f[:, 4:8, m, :], MT + m)

            def v_center(m):
                center(v_f[:, :, m, :], MT + m).then_inc(norm_done, 1)

            def v_lo_part(m):
                dve.wait_ge(v_hi_done, m + 1)
                nc.vector.tensor_tensor(v_lo[:, :, m, :], v_f[:, :, m, :], v_hi[:, :, m, :].bitcast(FP), ALU.subtract).then_inc(v_lo_done, 1)

            for i in range(U_V + 2, U_V + 9):
                w_lo(i)
            v_stats(0)
            v_stats(1)
            w_lo(U_V + 9)
            for m in range(4):
                v_center(m)
                if m < 2:
                    v_stats(m + 2)
                w_lo(U_V + 10 + m)
                v_lo_part(m)
            for i in range(U_V + 14, U_V + 17):
                w_lo(i)
            v_stats(4)
            v_stats(5)
            w_lo(U_U + 1)
            for m in range(4, MT):
                v_center(m)
                if m < 6:
                    v_stats(m + 2)
                if m > 4:
                    v_lo_part(m - 1)
            v_lo_part(MT - 1)

            def gate_head(h):
                for i in range(2):
                    wait_full(dve, ("mix", h, i))
                    s = slice(HALF * i, HALF * i + HALF)
                    link(nc.vector.scalar_tensor_tensor(
                        out=yb_f[:, h, s].rearrange("p (c t) -> p c t", t=P), in0=bank(("mix", h, i))[:].rearrange("p (c t) -> p c t", t=P),
                        scalar=cols[:, COL_G + h:COL_G + h + 1], in1=rr[:, h, :].unsqueeze(1).broadcast_to([P, 4, P]),
                        op0=ALU.mult, op1=ALU.add))
                    dve.sem_inc(free(("mix", h, i)), 1)
                dve.wait_ge(gu_done, 2 * h + 2)
                nc.vector.tensor_tensor(yb_f[:, h, :], yb_f[:, h, :], tt[h % 2][:, 0:S], ALU.mult).then_inc(yb_f_done, 1)

            def yb_lo_part(h):
                dve.wait_ge(yb_hi_done, h + 1)
                nc.vector.tensor_tensor(yb_lo[:, h, :], yb_f[:, h, :], yb_hi[:, h, :].bitcast(FP), ALU.subtract).then_inc(yb_lo_done, 1)

            for h in range(KT):
                w_lo(U_U + h + 2)
                gate_head(h)
                if h:
                    yb_lo_part(h - 1)
            yb_lo_part(KT - 1)

            def pb_merge(n):
                for i in range(2):
                    s = slice(HALF * i, HALF * i + HALF)
                    dve.wait_ge(sgb_done, 2 * n + i + 1)
                    wait_full(dve, ("pb", n, i))
                    link(nc.vector.tensor_tensor(tt[n % 2][:, s], tt[n % 2][:, s], bank(("pb", n, i))[:], ALU.mult))
                    dve.sem_inc(free(("pb", n, i)), 1)
                    nc.vector.tensor_tensor(am[:, n, s], am[:, n, s], tt[n % 2][:, s], ALU.add).then_inc(am_done, 1)

            def merged_lo(n):
                dve.wait_ge(mg_hi_done, n + 1)
                nc.vector.tensor_tensor(mT[:, :, 1, n, :], am[:, n, :].rearrange("p (m t) -> p m t", t=P),
                                        mT[:, :, 0, n, :].bitcast(FP), ALU.subtract).then_inc(mg_lo_done, 1)

            for i, (kind, n) in enumerate(GB_PB[:-2]):
                if kind == "pb":
                    pb_merge(n)
                w_lo(U_GP + i + 2)
            for k in range(3):
                merged_lo(2 * k)
                merged_lo(2 * k + 1)
                w_lo(U_WO + k)
            pb_merge(6)
            merged_lo(6)
            w_lo(U_WO + 3)
            pb_merge(7)
            w_lo(U_WO + 4)
            merged_lo(7)
            for k in range(5, KT):
                w_lo(U_WO + k)

            def residual(m):
                for j in range(2):
                    s = slice(HALF * j, HALF * j + HALF)
                    dve.wait_ge(h0_in[m], 16)
                    wait_full(dve, ("wo", m, j))
                    link(nc.vector.scalar_tensor_tensor(out=h1[:, m, s], in0=h1[:, m, s], scalar=ALPHA, in1=bank(("wo", m, j))[:],
                                                        op0=ALU.mult, op1=ALU.add))
                    dve.sem_inc(free(("wo", m, j)), 1)

            def softmax(m):
                wait_full(dve, ("lg", m))
                nc.vector.tensor_reduce(out=nmax[:], in_=bank(("lg", m))[:, 0:NE], axis=AX.X, op=ALU.max, negate=True).then_inc(nmax_done, 1)
                dve.wait_ge(exp_done, m + 1)
                link(nc.vector.reciprocal(rsum[:], esum[:]))
                nc.vector.tensor_scalar(aff[:, m, :], aff[:, m, :], rsum[:], None, ALU.mult).then_inc(aff_done, 1)

            dve.wait_ge(ln1_in, 32)
            for m in range(MT):
                if m == 3:
                    softmax(0)
                residual(m)
                stats(h1[:, m, 0:HALF], h1[:, m, HALF:D], 2 * MT + m)
                link(scale(h1[:, m, :], g1[:], 2 * MT + m))
                if m >= 3:
                    softmax(m - 2)
                affine(h1[:, m, :], b1[:], 2 * MT + m).then_inc(affine_dve, 1)
            softmax(6)
            softmax(7)

            dve.wait_ge(affT_done, MT)
            for r in range(CAP // 8):
                link(nc.vector.max(top8[:], affT[:]))
                link(nc.vector.match_replace(affT[:], top8[:], affT[:], -1.0))
            dve.wait_ge(aff_stored, 16)
            link(nc.vector.tensor_scalar(sel[:], affT[:], 0.0, None, ALU.is_lt))
            nc.vector.tensor_tensor_scan(cs_r[:], sel[:], sel[:], 0.0, ALU.add, ALU.max).then_inc(cs_r_done, 1)

            dve.wait_ge(e_lo_first, NSPLIT)
            dve.sem_inc(e_lo_done, NSPLIT)

            def token_numbers(e):
                dve.wait_ge(csb_in, 16 * e)
                nc.vector.tensor_scalar(csb[:], csb[:], slot_no[:], 0.0, ALU.is_le, ALU.add, accum_out=idx_f[:]).then_inc(dve_step, 1)

            for i in range(2):
                wait_full(dve, ("cb", i))
                ins = nc.vector.tensor_scalar(sil[:, i, :], bank(("cb", i))[:], slot_no[:], 0.0, ALU.is_le, ALU.add, accum_out=idx_h[:, i:i + 1])
                link(ins)
                dve.sem_inc(free(("cb", i)), 1)
            nc.vector.tensor_tensor(idx_g[:], idx_h[:, 0:1], idx_h[:, 1:2], ALU.add).then_inc(idx_done, 1)

            def x_lo(src, i, n):
                dve.wait_ge(xe_hi_done, n)
                nc.vector.tensor_tensor(flat(xeT_lo[:, 4 * i:4 * i + 4, :]), src, flat(xeT_hi[:, 4 * i:4 * i + 4, :]).bitcast(FP),
                                        ALU.subtract).then_inc(xe_lo_done, 1)
                dve.wait_ge(xe_lo_done, n)

            for i in range(2):
                x_lo(bank(("xt", i))[:], i, i + 1)
                dve.sem_inc(free(("xt", i)), 1)

            def e_lo(u, g):
                dve.wait_ge(e_hi_done, g + 1)
                nc.vector.tensor_tensor(el[u % NSPLIT][:], raw[:, raw_slot(u), :], eh[u % NSPLIT][:].bitcast(FP), ALU.subtract).then_inc(e_lo_done, 1)

            def hid_part(j, e):
                dve.wait_ge(sil_done, 4 * e + j + 1)
                e_wait_full(dve, ("u", j), e)
                nc.vector.tensor_tensor(hid[:, j % 2, :], sil[:, j % 2, :], ebank(("u", j))[:], ALU.mult).then_inc(hid_done, 1)
                dve.wait_ge(hid_done, 4 * e + j + 1)
                dve.sem_inc(e_free(("u", j)), 1)

            def hidT_lo_part(j, e):
                dve.wait_ge(hT2_hi_done, 4 * e + j + 1)
                nc.vector.tensor_tensor(flat(hidT_lo[:, 4 * j:4 * j + 4, :]), ebank(("t", j))[:],
                                        flat(hidT_hi[:, 4 * j:4 * j + 4, :]).bitcast(FP), ALU.subtract).then_inc(hT2_lo_done, 1)
                dve.wait_ge(hT2_lo_done, 4 * e + j + 1)
                dve.sem_inc(e_free(("t", j)), 1)

            base_steps = steps[0]

            def body(e, last):
                for u in range(NSPLIT, EU):
                    e_lo(u, EU * e + u)
                    if u in (6, 10, 14):
                        hid_part((u - 6) // 4, e)
                    if u in (10, 14, 18, 21):
                        hidT_lo_part((10, 14, 18, 21).index(u), e)
                    if u == 18:
                        hid_part(3, e)
                    if not last and u in (18, 21):
                        i = (18, 21).index(u)
                        x_lo(ebank(("x", i))[:], i, 2 * e + 3 + i)
                        dve.sem_inc(e_free(("x", i)), 1)
                    if not last and u == 4:
                        token_numbers(e + 1)
                        dve.wait_ge(dve_step, base_steps + e + 1)
                        dve.wait_ge(idx_m_done, e + 1)
                        nc.vector.tensor_copy(idx_g[:], idx_f[:]).then_inc(idx_done, 1)
                if not last:
                    for u in range(NSPLIT):
                        e_lo(u, EU * e + EU + u)

            with dve.Fori(0, NE - 1) as e:
                body(e, False)
            body(NE - 1, True)
            steps[0] += NE - 1

            dve.wait_ge(ln2_in, 32)
            for m in range(MT):
                dve.wait_ge(fin_in[m], 16)
                stats(fin[:, m, 0:HALF], fin[:, m, HALF:D], 3 * MT + m)
                if m < MT - 1:
                    scale(fin[:, m, :], g2[:], 3 * MT + m).then_inc(norm_done, 1)
            link(scale(fin[:, MT - 1, :], g2[:], 4 * MT - 1))
            affine(fin[:, MT - 1, :], b2[:], 4 * MT - 1).then_inc(affine_dve, 1)

        @block.tensor
        def _(pe):
            def three(dst, a_hi, a_lo, b_hi, b_lo, start, stop):
                nc.tensor.matmul(dst, a_hi, b_hi, start=start, stop=False)
                nc.tensor.matmul(dst, a_hi, b_lo, start=False, stop=False)
                return nc.tensor.matmul(dst, a_lo, b_hi, start=False, stop=stop)

            pe.wait_ge(ident_ok, 1)
            pe.wait_ge(vec_in, 64)
            nc.tensor.transpose(bank("cols")[:, 0:N_COLS], vec_rows[:], ident[0:N_COLS, 0:N_COLS]).then_inc(full("cols"), 1)

            def h_transpose(m):
                pe.wait_ge(affine_done, m + 1)
                for i in range(2):
                    wait_free(("h", m, i))
                    for k in range(4):
                        kk = 4 * i + k
                        last = nc.tensor.transpose(bank(("h", m, i))[:, P * k:P * k + P], xr[:, m, P * kk:P * kk + P], ident[:])
                    last.then_inc(full(("h", m, i)), 1)

            def project_half(i, name, n, half, a_kts, b_hi, b_lo, off=0, width=P):
                h3, l3 = (t.rearrange("p (k n) -> p k n", n=width) for t in halves(i))
                wait_free((name, n, half))
                for k in range(a_kts):
                    last = three(bank((name, n, half))[:], h3[:, k, off:off + P], l3[:, k, off:off + P],
                                 b_hi[:, k, HALF * half:HALF * half + HALF], b_lo[:, k, HALF * half:HALF * half + HALF],
                                 k == 0, k == a_kts - 1)
                last.then_inc(full((name, n, half)), 1)

            def project(i, name, n, a_kts, b_hi, b_lo, off=0, width=P):
                for half in range(2):
                    project_half(i, name, n, half, a_kts, b_hi, b_lo, off, width)

            def tile_rows(name, m, j, k, w, a_hi, a_lo, start):
                s = slice(HALF * j, HALF * j + HALF)
                return three(bank((name, m, j))[:], a_hi, a_lo, w[0][:, s], w[1][:, s], start, k == KT - 1)

            for m in range(4):
                h_transpose(m)
            pe.wait_ge(hT_lo_done, MT)
            for g in range(NG):
                pe.wait_ge(w_lo_done, U_A + g + 1)
                project_half(U_A + g, "a", g, 0, KT, hT_hi, hT_lo)
                h_transpose(4 + g)
            pe.wait_ge(hT_lo_done, 2 * MT)
            for g in range(NG):
                project_half(U_A + g, "a", g, 1, KT, hT_hi, hT_lo)
            for n in range(KT):
                pe.wait_ge(w_lo_done, U_GA + n + 1)
                project(U_GA + n, "ga", n, KT, hT_hi, hT_lo)
                if 2 <= n < 2 + NG:
                    g = n - 2
                    pe.wait_ge(pw_lo_done, 1)
                    pe.wait_ge(pa_lo_done, g + 1)
                    for i in range(2):
                        wait_free(("ya", g, i))
                        s = slice(HALF * i, HALF * i + HALF)
                        three(bank(("ya", g, i))[:], pw_hi[:, g, :], pw_lo[:, g, :], pa_hi[:, s], pa_lo[:, s],
                              True, True).then_inc(full(("ya", g, i)), 1)
            pe.wait_ge(ws_in, 16)
            for i in range(2):
                wait_free(("ws", i))
                for h in range(4):
                    last = nc.tensor.transpose(bank(("ws", i))[:, P * h:P * h + P], ws_raw[:, 4 * i + h, :], ident[:])
                last.then_inc(full(("ws", i)), 1)
            pe.wait_ge(ya_lo_done, 2 * NG)
            for n in range(KT):
                i = U_PA + n // 2
                pe.wait_ge(w_lo_done, i + 1)
                project(i, "pa", n, NG, ya_hi, ya_lo, off=P * (n % 2), width=2 * P)
                if n == 1:
                    pe.wait_ge(consts, 2)
                    for i in range(2):
                        pe.wait_ge(wsT_done, i + 1)
                        wait_free(("rw", i))
                        nc.tensor.matmul(bank(("rw", i))[:], ones[:], flat(wsT[:, 4 * i:4 * i + 4, :]), start=True, stop=True).then_inc(full(("rw", i)), 1)
            pe.wait_ge(ones_r_done, 1)
            pe.wait_ge(bv_done, 1)
            for grp in range(2):
                for k in range(KT):
                    i = U_V + 8 * grp + k
                    pe.wait_ge(w_lo_done, i + 1)
                    for m in range(4 * grp, 4 * grp + 4):
                        for j in range(2):
                            if k == 0:
                                wait_free(("v", m, j))
                                nc.tensor.matmul(bank(("v", m, j))[:], ones_r[:], bv[:, HALF * j:HALF * j + HALF], start=True, stop=False)
                            last = tile_rows("v", m, j, k, halves(i), hT_hi[:, k, P * m:P * m + P],
                                             hT_lo[:, k, P * m:P * m + P], False)
                            if k == KT - 1:
                                last.then_inc(full(("v", m, j)), 1)
                    if k < KT - 1:
                        last.then_inc(w_used, 1)

            def u_head(h):
                pe.wait_ge(w_lo_done, U_U + h + 1)
                project(U_U + h, "u", h, KT, hT_hi, hT_lo)

            u_head(0)
            for h in range(KT):
                if h + 1 < KT:
                    u_head(h + 1)
                pe.wait_ge(v_lo_done, MT)
                for i in range(2):
                    wait_free(("mix", h, i))
                    for c in range(4):
                        m = 4 * i + c
                        last = three(bank(("mix", h, i))[:, P * c:P * c + P], v_hi[:, h, m, :], v_lo[:, h, m, :],
                                     ws_hi[:, h, :], ws_lo[:, h, :], True, True)
                    last.then_inc(full(("mix", h, i)), 1)
            for i, (kind, n) in enumerate(GB_PB):
                pe.wait_ge(w_lo_done, U_GP + i + 1)
                if kind == "gb":
                    project(U_GP + i, "gb", n, KT, hT_hi, hT_lo)
                else:
                    if n == 0:
                        pe.wait_ge(yb_lo_done, KT)
                    project(U_GP + i, "pb", n, KT, yb_hi, yb_lo)
            for k in range(KT):
                pe.wait_ge(w_lo_done, U_WO + k + 1)
                pe.wait_ge(mg_lo_done, k + 1)
                for m in range(2):
                    for j in range(2):
                        if k == 0:
                            wait_free(("wo", m, j))
                        last = tile_rows("wo", m, j, k, halves(U_WO + k), mT[:, m, 0, k, :], mT[:, m, 1, k, :], k == 0)
                        if k == KT - 1:
                            last.then_inc(full(("wo", m, j)), 1)

            pe.wait_ge(rt_in, 16)
            for step in route_steps:
                kind, m = step[0], step[1]
                if kind == "wo":
                    wait_free(step)
                    for k in range(KT):
                        last = tile_rows("wo", m, step[2], k, halves(U_WO + k), mT[:, m, 0, k, :], mT[:, m, 1, k, :], k == 0)
                    last.then_inc(full(step), 1)
                elif kind == "t":
                    pe.wait_ge(affine_dve, m + 1)
                    for i in range(2):
                        wait_free(("t", m, i))
                        for k in range(4):
                            kk = 4 * i + k
                            last = nc.tensor.transpose(bank(("t", m, i))[:, P * k:P * k + P], h1[:, m, P * kk:P * kk + P], ident[:])
                        last.then_inc(full(("t", m, i)), 1)
                elif kind == "lg":
                    wait_free(step)
                    for k in range(KT):
                        if k % 4 == 0:
                            pe.wait_ge(h1T_done, 2 * m + 1 + k // 4)
                        last = nc.tensor.matmul(bank(step)[:, 0:NE], h1T[:, m % 2, k, :], w_rt[:, k, :], start=(k == 0), stop=(k == KT - 1))
                    last.then_inc(full(step), 1)
                else:
                    pe.wait_ge(aff_done, m + 1)
                    wait_free(step)
                    nc.tensor.transpose(bank(step)[0:NE, 0:P], aff[:, m, :], ident[:]).then_inc(full(step), 1)

            pe.wait_ge(cs_r_done, 1)
            for i in range(2):
                wait_free(("cb", i))
                nc.tensor.matmul(bank(("cb", i))[:], ones_r[0:1, :], cs_r[0:1, HALF * i:HALF * i + HALF], start=True, stop=True).then_inc(full(("cb", i)), 1)

            pe.wait_ge(gathered, 16)
            for i in range(2):
                wait_free(("xt", i))
                for k in range(4):
                    kk = 4 * i + k
                    last = nc.tensor.transpose(bank(("xt", i))[:, P * k:P * k + P], xe[:, P * kk:P * kk + P], ident[:])
                last.then_inc(full(("xt", i)), 1)

            def gate_up(j, e):
                for half in range(4):
                    u = 4 * j + half
                    name = ("gu"[half // 2], j)
                    pe.wait_ge(e_lo_done, EU * e + u + 1)
                    if half % 2 == 0:
                        e_wait_free(name, e)
                    h3 = eh[u % NSPLIT][:].rearrange("p (k f) -> p k f", k=4)
                    l3 = el[u % NSPLIT][:].rearrange("p (k f) -> p k f", k=4)
                    for k in range(4):
                        kk = 4 * (half % 2) + k
                        last = three(ebank(name)[:], xeT_hi[:, kk, :], xeT_lo[:, kk, :], h3[:, k, :], l3[:, k, :], kk == 0, kk == KT - 1)
                    last.then_inc(e_used if half % 2 == 0 else e_full(name), 1)

            def hid_transpose(j, e):
                pe.wait_ge(hid_done, 4 * e + j + 1)
                e_wait_free(("t", j), e)
                for k in range(4):
                    last = nc.tensor.transpose(ebank(("t", j))[:, P * k:P * k + P], hid[:, j % 2, P * k:P * k + P], ident[:])
                last.then_inc(e_full(("t", j)), 1)

            def next_tokens(i, e):
                pe.wait_ge(gathered, 16 * e + 32)
                e_wait_free(("x", i), e)
                for k in range(4):
                    kk = 4 * i + k
                    last = nc.tensor.transpose(ebank(("x", i))[:, P * k:P * k + P], xe[:, P * kk:P * kk + P], ident[:])
                last.then_inc(e_full(("x", i)), 1)

            def down(u, e):
                pe.wait_ge(e_lo_done, EU * e + u + 1)
                h3 = eh[u % NSPLIT][:].rearrange("p (k n) -> p k n", k=2)
                l3 = el[u % NSPLIT][:].rearrange("p (k n) -> p k n", k=2)
                for k in range(2):
                    kk = 2 * (u - 16) + k
                    for j in range(2):
                        s = slice(HALF * j, HALF * j + HALF)
                        last = three(ebank(("d", j))[:], hidT_hi[:, kk, :], hidT_lo[:, kk, :], h3[:, k, s], l3[:, k, s],
                                     kk == 0, kk == F // P - 1)
                        if u == EU - 1 and k == 1:
                            last.then_inc(e_full(("d", j)), 1)
                if u < EU - 1:
                    last.then_inc(e_used, 1)

            def body(e, last):
                pe.wait_ge(xe_lo_done, 2 * e + 2)
                gate_up(0, e)
                gate_up(1, e)
                hid_transpose(0, e)
                gate_up(2, e)
                hid_transpose(1, e)
                gate_up(3, e)
                hid_transpose(2, e)
                if not last:
                    next_tokens(0, e)
                pe.wait_ge(hT2_lo_done, 4 * e + 1)
                e_wait_free(("d", 0), e)
                e_wait_free(("d", 1), e)
                down(16, e)
                down(17, e)
                hid_transpose(3, e)
                if not last:
                    next_tokens(1, e)
                for u in range(18, EU):
                    if u % 2 == 0:
                        pe.wait_ge(hT2_lo_done, 4 * e + (u - 16) // 2 + 1)
                    down(u, e)

            with pe.Fori(0, NE - 1) as e:
                body(e, False)
            body(NE - 1, True)


_INS = ["x", "in_ln_g", "in_ln_b", "w_in", "b_in", "pool_w", "pool_scale", "sgu_ln_g", "sgu_ln_b", "sgu_w", "sgu_b",
        "p_a", "p_b", "w_out", "ln1_g", "ln1_b", "w_router", "w_gate", "w_up", "w_down", "ln2_g", "ln2_b"]


def kernel(**inputs):
    import numpy as _np
    import concourse.bacc as _bacc
    from concourse import mybir as _mybir
    from concourse.bass_utils import run_bass_kernel_spmd as _run

    nc = _bacc.Bacc("TRN2", target_bir_lowering=False, num_devices=1)
    arrays, args = {}, []
    for name in _INS:
        a = _np.ascontiguousarray(inputs[name])
        arrays[f"in_{name}_dram"] = a
        args.append(nc.dram_tensor(f"in_{name}_dram", a.shape, _mybir.dt.from_np(a.dtype), kind="ExternalInput").ap())
    args.append(nc.dram_tensor("out_0_dram", (1, S, D), _mybir.dt.float32, kind="ExternalOutput").ap())
    hybrid_moe_kernel(nc, *args)
    r = _run(nc, [arrays], core_ids=[0])
    return r.results[0]["out_0_dram"]
```
